# Optimizing a Trainium2 kernel written in Bass

```python
import math
import jax, jax.numpy as jnp
from jax import lax
import numpy as np

D_MODEL = 1024
BATCH = 1
SEQ = 512
DEPTH = 2

EXPAND = 2
D_MIX = EXPAND * D_MODEL
D_CONV = D_MIX // 2
D_RET = D_MIX - D_CONV
CONV_GROUPS = 8
CONV_K = 3
RET_HEADS = 8
RET_HEAD_DIM = D_RET // RET_HEADS
CHUNK = 128
ROPE_BASE = 10000.0
NORM_EPS = 1e-6
IN_COLS = 4 * D_CONV + 4 * D_RET


def rms_norm(x, g, eps=NORM_EPS):
    xf = x.astype(jnp.float32)
    y = xf * lax.rsqrt(jnp.mean(xf * xf, axis=-1, keepdims=True) + eps)
    return (y * g.astype(jnp.float32)).astype(x.dtype)

def rotary_tables(positions):
    half = RET_HEAD_DIM // 2
    inv_freq = 1.0 / (ROPE_BASE ** (jnp.arange(half, dtype=jnp.float32) / half))
    ang = positions.astype(jnp.float32)[..., None] * inv_freq
    return jnp.cos(ang)[:, :, None, :], jnp.sin(ang)[:, :, None, :]

def apply_rotary(x, cos, sin):
    xf = x.astype(jnp.float32)
    x1, x2 = jnp.split(xf, 2, axis=-1)
    return jnp.concatenate([x1 * cos - x2 * sin, x2 * cos + x1 * sin], axis=-1).astype(x.dtype)

def causal_depthwise_conv(u, w):
    c = u.shape[-1]
    return lax.conv_general_dilated(
        u, w.astype(u.dtype)[:, None, :], window_strides=(1,), padding=[(CONV_K - 1, 0)],
        dimension_numbers=("NWC", "WIO", "NWC"), feature_group_count=c)

def retention_chunkwise(q, k, v, log_gamma):
    b, s, h, dh = q.shape
    n = s // CHUNK
    q = q.reshape(b, n, CHUNK, h, dh)
    k = k.reshape(b, n, CHUNK, h, dh) * (dh ** -0.5)
    v = v.reshape(b, n, CHUNK, h, dh)
    idx = jnp.arange(CHUNK, dtype=jnp.float32)
    diff = idx[:, None] - idx[None, :]
    causal = diff >= 0
    decay = jnp.where(causal[None], jnp.exp(log_gamma[:, None, None] * jnp.where(causal, diff, 0.0)[None]), 0.0)
    scores = jnp.einsum("bnihd,bnjhd->bnhij", q, k).astype(jnp.float32) * decay
    intra = jnp.einsum("bnhij,bnjhe->bnihe", scores, v.astype(jnp.float32))
    k_w = jnp.exp((CHUNK - 1 - idx)[:, None] * log_gamma[None, :])
    kv = jnp.einsum("bnjhd,bnjhe->nbhde", k.astype(jnp.float32) * k_w[:, :, None],
                    v.astype(jnp.float32))
    chunk_decay = jnp.exp(CHUNK * log_gamma)[None, :, None, None]

    def step(state, kv_n):
        return chunk_decay * state + kv_n, state

    init = jnp.zeros((b, h, dh, dh), jnp.float32)
    _, prev = lax.scan(step, init, kv)
    q_w = jnp.exp((idx + 1.0)[:, None] * log_gamma[None, :])
    cross = jnp.einsum("bnihd,nbhde->bnihe", q.astype(jnp.float32) * q_w[:, :, None], prev)
    return (intra + cross).reshape(b, s, h, dh)

def first_inputs(seed: int = 0) -> dict:
    key = jax.random.key(seed)
    kx, kp, kn1, kw1, kc, kw2, kn2 = jax.random.split(key, 7)
    x = jax.random.normal(kx, (BATCH, SEQ, D_MODEL), jnp.float32)
    offsets = jax.random.randint(kp, (BATCH, 1), 0, 1024, dtype=jnp.int32)
    positions = offsets + jnp.arange(SEQ, dtype=jnp.int32)[None, :]
    pre_norm = 1.0 + 0.05 * jax.random.normal(kn1, (DEPTH, D_MODEL), jnp.float32)
    w_in = jax.random.normal(kw1, (DEPTH, D_MODEL, IN_COLS), jnp.float32) * D_MODEL ** -0.5
    conv_w = jax.random.normal(kc, (DEPTH, CONV_K, D_CONV), jnp.float32) * CONV_K ** -0.5
    w_out = jax.random.normal(kw2, (DEPTH, D_MIX, D_MODEL), jnp.float32) * D_MIX ** -0.5
    post_norm = 1.0 + 0.05 * jax.random.normal(kn2, (DEPTH, D_MODEL), jnp.float32)
    return {"x": x, "positions": positions, "pre_norm": pre_norm, "w_in": w_in,
            "conv_w": conv_w, "w_out": w_out, "post_norm": post_norm}

def first_block(x, positions, pre_norm, w_in, conv_w, w_out, post_norm):
    b, s, _ = x.shape
    cos, sin = rotary_tables(positions)
    log_gamma = jnp.log1p(-jnp.exp2(-5.0 - jnp.arange(RET_HEADS, dtype=jnp.float32)))
    cuts = [D_CONV, 2 * D_CONV, 3 * D_CONV, 4 * D_CONV,
            4 * D_CONV + D_RET, 4 * D_CONV + 2 * D_RET, 4 * D_CONV + 3 * D_RET]
    for layer in range(DEPTH):
        h = rms_norm(x, pre_norm[layer])
        proj = jnp.einsum("bsd,dp->bsp", h, w_in[layer])
        c_b, c_c, c_x, c_z, r_q, r_k, r_v, r_z = jnp.split(proj, cuts, axis=-1)
        y_conv = c_b * causal_depthwise_conv(c_c * c_x, conv_w[layer])
        y_conv = y_conv * jax.nn.silu(c_z)
        q = apply_rotary(r_q.reshape(b, s, RET_HEADS, RET_HEAD_DIM), cos, sin)
        k = apply_rotary(r_k.reshape(b, s, RET_HEADS, RET_HEAD_DIM), cos, sin)
        v = r_v.reshape(b, s, RET_HEADS, RET_HEAD_DIM)
        ret = retention_chunkwise(q, k, v, log_gamma)
        ret = ret * lax.rsqrt(jnp.mean(ret * ret, axis=-1, keepdims=True) + NORM_EPS)
        y_ret = ret.reshape(b, s, D_RET).astype(h.dtype) * jax.nn.silu(r_z)
        mix = jnp.concatenate([y_conv.astype(h.dtype), y_ret], axis=-1)
        out = jnp.einsum("bse,ed->bsd", mix, w_out[layer])
        x = x + rms_norm(out, post_norm[layer]).astype(x.dtype)
    return x


N_META = 16
EPS = 1e-6
SSD_D_INNER = 2 * D_MODEL
SSD_HEAD_DIM = 64
SSD_HEADS = SSD_D_INNER // SSD_HEAD_DIM
SSD_GROUPS = 8
SSD_HPG = SSD_HEADS // SSD_GROUPS
SSD_STATE = 128
SSD_CONV = 4
SSD_CHUNK = 128
SSD_CONV_DIM = SSD_D_INNER + 2 * SSD_GROUPS * SSD_STATE
SSD_IN_DIM = SSD_D_INNER + SSD_CONV_DIM + SSD_HEADS
MLA_HEADS = 16
MLA_NOPE = 64
MLA_ROPE = 32
MLA_V = 64
MLA_QK = MLA_NOPE + MLA_ROPE
MLA_Q_RANK = 384
MLA_KV_RANK = 256
MLA_IN_DIM = MLA_Q_RANK + MLA_KV_RANK + MLA_ROPE
ROPE_THETA = 10000.0
ATTN_BLOCK = 128
D_FF = 4 * D_MODEL
N_SSD_LAYERS = (DEPTH + 1) // 2
N_MLA_LAYERS = DEPTH // 2


def rms_norm_2(x, gain):
    xf = x.astype(jnp.float32)
    y = xf * lax.rsqrt(jnp.mean(xf * xf, axis=-1, keepdims=True) + EPS)
    return (y * gain.astype(jnp.float32)).astype(x.dtype)

def causal_depthwise_conv_2(u, w, b):
    out = lax.conv_general_dilated(
        u, w[:, None, :].astype(u.dtype), window_strides=(1,),
        padding=[(SSD_CONV - 1, 0)], dimension_numbers=('NWC', 'WIO', 'NWC'),
        feature_group_count=u.shape[-1])
    return out + b.astype(u.dtype)

def ssd_mixer(h, w_in, conv_w, conv_b, dt_bias, a_log, d_skip, norm_g, w_out):
    f32 = jnp.float32
    bsz, L, _ = h.shape
    zxbcdt = h @ w_in
    z, xbc, dt = jnp.split(zxbcdt, [SSD_D_INNER, SSD_D_INNER + SSD_CONV_DIM], axis=-1)
    xbc = jax.nn.silu(causal_depthwise_conv_2(xbc, conv_w, conv_b))
    xs, b_in, c_in = jnp.split(xbc, [SSD_D_INNER, SSD_D_INNER + SSD_GROUPS * SSD_STATE], axis=-1)
    dt = jax.nn.softplus(dt.astype(f32) + dt_bias.astype(f32))
    a = -jnp.exp(a_log.astype(f32))

    pad = (-L) % SSD_CHUNK
    n_chunks = (L + pad) // SSD_CHUNK

    def front_pad(t):
        return jnp.pad(t.astype(f32), [(0, 0), (pad, 0)] + [(0, 0)] * (t.ndim - 2))

    x_c = front_pad(xs).reshape(bsz, n_chunks, SSD_CHUNK, SSD_GROUPS, SSD_HPG, SSD_HEAD_DIM)
    b_c = front_pad(b_in).reshape(bsz, n_chunks, SSD_CHUNK, SSD_GROUPS, SSD_STATE)
    c_c = front_pad(c_in).reshape(bsz, n_chunks, SSD_CHUNK, SSD_GROUPS, SSD_STATE)
    dt_c = front_pad(dt).reshape(bsz, n_chunks, SSD_CHUNK, SSD_GROUPS, SSD_HPG)
    xdt = x_c * dt_c[..., None]
    a_dt = (dt_c * a.reshape(SSD_GROUPS, SSD_HPG)).transpose(0, 1, 3, 4, 2)
    a_cs = jnp.cumsum(a_dt, axis=-1)

    idx = jnp.arange(SSD_CHUNK)
    causal = idx[:, None] >= idx[None, :]
    decay = jnp.exp(jnp.where(causal, a_cs[..., :, None] - a_cs[..., None, :], -jnp.inf))
    cb = jnp.einsum('bclgn,bcsgn->bcgls', c_c, b_c)
    y_diag = jnp.einsum('bcgjls,bcsgjp->bclgjp', cb[:, :, :, None] * decay, xdt)

    decay_to_end = jnp.exp(a_cs[..., -1:] - a_cs).transpose(0, 1, 4, 2, 3)
    states = jnp.einsum('bclgn,bclgjp->bcgjpn', b_c, xdt * decay_to_end[..., None])
    chunk_decay = jnp.exp(a_cs[..., -1])

    def step(carry, inp):
        st, dec = inp
        return carry * dec[..., None, None] + st, carry

    init = jnp.zeros((bsz, SSD_GROUPS, SSD_HPG, SSD_HEAD_DIM, SSD_STATE), f32)
    _, prev = lax.scan(step, init, (jnp.moveaxis(states, 1, 0), jnp.moveaxis(chunk_decay, 1, 0)))
    prev = jnp.moveaxis(prev, 0, 1)
    decay_from_start = jnp.exp(a_cs).transpose(0, 1, 4, 2, 3)
    y_off = jnp.einsum('bclgn,bcgjpn->bclgjp', c_c, prev) * decay_from_start[..., None]

    y = (y_diag + y_off).reshape(bsz, n_chunks * SSD_CHUNK, SSD_D_INNER)[:, pad:]
    y = y + xs.astype(f32) * jnp.repeat(d_skip.astype(f32), SSD_HEAD_DIM)
    g = (y * jax.nn.silu(z.astype(f32))).reshape(bsz, L, SSD_GROUPS, SSD_D_INNER // SSD_GROUPS)
    g = g * lax.rsqrt(jnp.mean(g * g, axis=-1, keepdims=True) + EPS)
    g = g.reshape(bsz, L, SSD_D_INNER) * norm_g.astype(f32)
    return g.astype(h.dtype) @ w_out

def rope_tables(L):
    inv = 1.0 / (ROPE_THETA ** (jnp.arange(0, MLA_ROPE, 2, dtype=jnp.float32) / MLA_ROPE))
    ang = jnp.arange(L, dtype=jnp.float32)[:, None] * inv[None, :]
    return jnp.cos(ang)[None, :, None, :], jnp.sin(ang)[None, :, None, :]

def apply_rope(t, cos, sin):
    t1, t2 = jnp.split(t, 2, axis=-1)
    cos = cos.astype(t.dtype)
    sin = sin.astype(t.dtype)
    return jnp.concatenate([t1 * cos - t2 * sin, t1 * sin + t2 * cos], axis=-1)

def mla_mixer(h, w_in, q_a_g, w_q_b, kv_a_g, w_kv_b, q_norm_g, k_norm_g, w_out):
    bsz, L, _ = h.shape
    q_lat, kv_lat, k_pe = jnp.split(h @ w_in, [MLA_Q_RANK, MLA_Q_RANK + MLA_KV_RANK], axis=-1)
    q = (rms_norm_2(q_lat, q_a_g) @ w_q_b).reshape(bsz, L, MLA_HEADS, MLA_QK)
    kv = (rms_norm_2(kv_lat, kv_a_g) @ w_kv_b).reshape(bsz, L, MLA_HEADS, MLA_NOPE + MLA_V)
    k_nope, v = jnp.split(kv, [MLA_NOPE], axis=-1)
    k = jnp.concatenate(
        [k_nope, jnp.broadcast_to(k_pe[:, :, None, :], (bsz, L, MLA_HEADS, MLA_ROPE))], axis=-1)
    q = rms_norm_2(q, q_norm_g)
    k = rms_norm_2(k, k_norm_g)
    cos, sin = rope_tables(L)
    q = jnp.concatenate([q[..., :MLA_NOPE], apply_rope(q[..., MLA_NOPE:], cos, sin)], axis=-1)
    k = jnp.concatenate([k[..., :MLA_NOPE], apply_rope(k[..., MLA_NOPE:], cos, sin)], axis=-1)
    scale = MLA_QK ** -0.5

    blocks = [(0, N_META)] + [(s, min(s + ATTN_BLOCK, L)) for s in range(N_META, L, ATTN_BLOCK)]
    outs = []
    for s, e in blocks:
        sc = jnp.einsum('bqhd,bkhd->bhqk', q[:, s:e], k[:, :e]).astype(jnp.float32) * scale
        mask = jnp.arange(e)[None, :] <= jnp.arange(s, e)[:, None]
        p = jax.nn.softmax(jnp.where(mask, sc, -jnp.inf), axis=-1).astype(v.dtype)
        outs.append(jnp.einsum('bhqk,bkhd->bqhd', p, v[:, :e]))
    o = jnp.concatenate(outs, axis=1).reshape(bsz, L, MLA_HEADS * MLA_V)
    return o @ w_out

def sqrelu_mlp(h, w_up, w_down):
    return jnp.square(jax.nn.relu(h @ w_up)) @ w_down

def second_inputs(seed: int = 0) -> dict:
    key = jax.random.key(seed)
    ks = jax.random.split(key, 24)
    f32 = jnp.float32

    def nrm(k, shape, fan_in):
        return jax.random.normal(k, shape, f32) * (fan_in ** -0.5)

    def gain(k, shape):
        return 1.0 + 0.02 * jax.random.normal(k, shape, f32)

    ns, nm = N_SSD_LAYERS, N_MLA_LAYERS
    dt0 = jnp.exp(jax.random.uniform(ks[7], (ns, SSD_HEADS), f32, np.log(1e-3), np.log(1e-1)))
    return {
        "x": jax.random.normal(ks[0], (BATCH, SEQ, D_MODEL), f32),
        "meta_tokens": jax.random.normal(ks[1], (N_META, D_MODEL), f32),
        "ln_mix": gain(ks[2], (DEPTH, D_MODEL)),
        "ln_mlp": gain(ks[3], (DEPTH, D_MODEL)),
        "ssd_w_in": nrm(ks[4], (ns, D_MODEL, SSD_IN_DIM), D_MODEL),
        "ssd_conv_w": nrm(ks[5], (ns, SSD_CONV, SSD_CONV_DIM), SSD_CONV),
        "ssd_conv_b": 0.02 * jax.random.normal(ks[6], (ns, SSD_CONV_DIM), f32),
        "ssd_dt_bias": dt0 + jnp.log(-jnp.expm1(-dt0)),
        "ssd_a_log": jnp.log(jax.random.uniform(ks[8], (ns, SSD_HEADS), f32, 1.0, 16.0)),
        "ssd_d": 1.0 + 0.1 * jax.random.normal(ks[9], (ns, SSD_HEADS), f32),
        "ssd_norm": gain(ks[10], (ns, SSD_D_INNER)),
        "ssd_w_out": nrm(ks[11], (ns, SSD_D_INNER, D_MODEL), SSD_D_INNER),
        "mla_w_in": nrm(ks[12], (nm, D_MODEL, MLA_IN_DIM), D_MODEL),
        "mla_q_a_norm": gain(ks[13], (nm, MLA_Q_RANK)),
        "mla_w_q_b": nrm(ks[14], (nm, MLA_Q_RANK, MLA_HEADS * MLA_QK), MLA_Q_RANK),
        "mla_kv_a_norm": gain(ks[15], (nm, MLA_KV_RANK)),
        "mla_w_kv_b": nrm(ks[16], (nm, MLA_KV_RANK, MLA_HEADS * (MLA_NOPE + MLA_V)), MLA_KV_RANK),
        "mla_q_norm": gain(ks[17], (nm, MLA_QK)),
        "mla_k_norm": gain(ks[18], (nm, MLA_QK)),
        "mla_w_out": nrm(ks[19], (nm, MLA_HEADS * MLA_V, D_MODEL), MLA_HEADS * MLA_V),
        "mlp_w_up": nrm(ks[20], (DEPTH, D_MODEL, D_FF), D_MODEL),
        "mlp_w_down": nrm(ks[21], (DEPTH, D_FF, D_MODEL), D_FF),
    }

def second_block(x, meta_tokens, ln_mix, ln_mlp, ssd_w_in, ssd_conv_w, ssd_conv_b, ssd_dt_bias,
              ssd_a_log, ssd_d, ssd_norm, ssd_w_out, mla_w_in, mla_q_a_norm, mla_w_q_b,
              mla_kv_a_norm, mla_w_kv_b, mla_q_norm, mla_k_norm, mla_w_out, mlp_w_up, mlp_w_down):
    bsz = x.shape[0]
    meta = jnp.broadcast_to(meta_tokens[None].astype(x.dtype), (bsz, N_META, D_MODEL))
    h = jnp.concatenate([meta, x], axis=1)
    for i in range(DEPTH):
        j = i // 2
        hn = rms_norm_2(h, ln_mix[i])
        if i % 2 == 0:
            h = h + ssd_mixer(hn, ssd_w_in[j], ssd_conv_w[j], ssd_conv_b[j], ssd_dt_bias[j],
                              ssd_a_log[j], ssd_d[j], ssd_norm[j], ssd_w_out[j])
        else:
            h = h + mla_mixer(hn, mla_w_in[j], mla_q_a_norm[j], mla_w_q_b[j], mla_kv_a_norm[j],
                              mla_w_kv_b[j], mla_q_norm[j], mla_k_norm[j], mla_w_out[j])
        h = h + sqrelu_mlp(rms_norm_2(h, ln_mlp[i]), mlp_w_up[i], mlp_w_down[i])
    return h[:, N_META:]


def setup_inputs(seed=0):
    out = dict(first_inputs(seed))
    for name, value in second_inputs(seed + 1).items():
        if name != "x":
            out[name + "_2"] = value
    return out


def reference(
    x, positions, pre_norm, w_in, conv_w, w_out, post_norm, meta_tokens_2, ln_mix_2, ln_mlp_2,
    ssd_w_in_2, ssd_conv_w_2, ssd_conv_b_2, ssd_dt_bias_2, ssd_a_log_2, ssd_d_2, ssd_norm_2,
    ssd_w_out_2, mla_w_in_2, mla_q_a_norm_2, mla_w_q_b_2, mla_kv_a_norm_2, mla_w_kv_b_2,
    mla_q_norm_2, mla_k_norm_2, mla_w_out_2, mlp_w_up_2, mlp_w_down_2,
):
    x = first_block(
        x, positions, pre_norm, w_in, conv_w, w_out, post_norm,
    )
    return second_block(
        x, meta_tokens_2, ln_mix_2, ln_mlp_2, ssd_w_in_2, ssd_conv_w_2, ssd_conv_b_2,
        ssd_dt_bias_2, ssd_a_log_2, ssd_d_2, ssd_norm_2, ssd_w_out_2, mla_w_in_2,
        mla_q_a_norm_2, mla_w_q_b_2, mla_kv_a_norm_2, mla_w_kv_b_2, mla_q_norm_2, mla_k_norm_2,
        mla_w_out_2, mlp_w_up_2, mlp_w_down_2,
    )


_drawn_inputs = setup_inputs


def setup_inputs(seed=0):
    import zlib

    import numpy as np

    out = dict(_drawn_inputs(seed))
    spreads = {}
    factors = {'ln_mix_2': 3.541,
     'ln_mlp_2': 3.41,
     'ssd_conv_b_2': 3.505,
     'ssd_norm_2': 5.149,
     'mla_q_a_norm_2': 8.0,
     'mla_kv_a_norm_2': 8.0,
     'mla_q_norm_2': 8.0,
     'mla_k_norm_2': 8.0,
     'ssd_d_2': 4.262}
    for name, (base, spread) in spreads.items():
        noise = np.random.default_rng([zlib.crc32(name.encode()), seed]).standard_normal(out[name].shape)
        drawn = base * np.exp(spread * noise) if base else spread * noise
        out[name] = __import__('jax').numpy.asarray(drawn.astype(out[name].dtype))
    for name, factor in factors.items():
        out[name] = (out[name] * factor).astype(out[name].dtype)
    return out
```

```python
import numpy as np

import concourse.bass as bass
from concourse import mybir
from concourse.alu_op_type import AluOpType as ALU

F32 = mybir.dt.float32
F32R = mybir.dt.float32r
BF16 = mybir.dt.bfloat16
I32 = mybir.dt.int32
ACT = mybir.ActivationFunctionType
AX_X = mybir.AxisListType.X

P = 128
D = 1024
KT = D // P
SEQ = 512
NOPE, ROPE = 64, 32
QK = NOPE + ROPE
META = 16
L = META + SEQ
HALF = L // 2
LAYERS1 = 2
HEADS1 = 8
EPS = 1e-6

ITER1 = 8
LAYER1 = HEADS1 * ITER1 + 2 * KT
GROUPS = 8
GROUP = 6
QUARTERS = 4
MLP = QUARTERS * 2 * KT
U_DT = LAYERS1 * LAYER1
U_SSD = U_DT + 1
U_SSD_OUT = U_SSD + GROUPS * GROUP
U_MLP0 = U_SSD_OUT + 2 * KT
U_MLA = U_MLP0 + MLP
U_MLA_V = U_MLA + 6
U_PAIR = U_MLA_V + 2
PAIRS = 8
U_MLA_OUT = U_PAIR + PAIRS
U_MLP1 = U_MLA_OUT + KT
UNITS = U_MLP1 + MLP
LEAD = 3

WIDE1 = [SEQ - P * j for j in range(SEQ // P)]
OFF1 = [sum(WIDE1[:j]) for j in range(len(WIDE1))]
TILES = [min(P, L - P * j) for j in range(-(-L // P))]
WIDE = [L - P * j for j in range(len(TILES))]
OFF = [sum(WIDE[:j]) for j in range(len(WIDE))]
NT = len(TILES)
CAUSAL = sum(WIDE)

RSQRT_LAYER = HEADS1 + 2
RSQRT_GROUPS = LAYERS1 * RSQRT_LAYER + 1
RSQRT_LATENT = RSQRT_GROUPS + GROUPS + 2
RSQRT_HEADS = RSQRT_LATENT + 2


def rsqrt_norm(n):
    if isinstance(n, int) and n >= LAYERS1:
        return {2: RSQRT_GROUPS, 3: RSQRT_LATENT - 1, 4: RSQRT_LATENT,
                5: RSQRT_HEADS + 2 * PAIRS + 1}[n]
    return RSQRT_LAYER * n + 1


COLS = {}


def _place_cols():
    at = 0
    for name, n in (("pre", LAYERS1 * KT), ("post", LAYERS1 * KT), ("conv", LAYERS1 * 3 * KT),
                    ("ln_mix", 2 * KT), ("ln_mlp", 2 * KT), ("inv_freq", 1), ("sin_sign", 1),
                    ("eps", 1), ("ssd_conv", 32 * 4), ("ssd_bias", 32), ("dt_bias", 1),
                    ("a_log", 1), ("ssd_d", 16), ("ssd_norm", 16), ("q_a", 3), ("kv_a", 2),
                    ("q_norm", 1), ("k_norm", 2)):
        COLS[name] = at
        at += n
    return at


N_COLS = _place_cols()

TWO_PI = (6.28125, 0.0019350051879882812, 2 * np.pi - 6.28125 - 0.0019350051879882812)
ROUND = 1.5 * 2.0 ** 23
PI_BELOW = 3.1415925


AHEAD = 1
AHEAD_MORE = {"decayed": 1, "o_sq": 1, "ossq": 1, "relu": 1, "silu": 1, "z2": 1, "cb": 1,
              "decay2": 3, "y_part": 3, "add": 1, "p_turned": 1, "pv": 1}
DMA_EVENTS = ("load0", "load1", "const", "pos", "cols", "x", "decay", "table", "stored")


def halves(t):
    return t.rearrange("p (a c) -> p a c", a=2)


LATER = ("z2", "o", "hidden_hi", "hidden", "relu", "relu_sq", "lifted", "mix_hi", "mix", "v", "v_t",
         "c", "cz", "rz", "ret_sq", "decayed", "sq", "o_sq")


class Build:

    def __init__(self, nc, ins, out):
        self.nc, self.ins, self.out = nc, ins, out
        self.signals = {}
        self.top = -(-nc.sbuf_base // 32) * 32
        self.resid = self.sbuf("resid", [P, KT, L])
        self.base = self.top
        self.o = self.sbuf("o", [P, KT, SEQ], at=self.base)
        self.h_hi = self.sbuf("h_hi", [P, KT, L], F32R)
        self.h_lo_at = self.top
        self.h_lo = self.sbuf("h_lo", [P, KT, L], F32R)
        self.mix_hi = self.sbuf("mix_hi", [P, 2 * KT, L], F32R)
        self.mix_lo = self.sbuf("mix_lo", [P, 2 * KT, L], F32R)
        self.w_raw = self.sbuf("w_raw", [P, 2, 8 * P])
        self.w_hi = self.sbuf("w_hi", [P, 4, 8 * P], F32R)
        self.w_lo = self.sbuf("w_lo", [P, 4, 8 * P], F32R)
        self.cols = self.sbuf("cols", [P, N_COLS])
        self.ident = self.sbuf("ident", [P, P])
        self.ones = self.sbuf("ones", [P, P])
        self.ident16 = self.sbuf("ident16", [P, P], BF16)
        self.mask_t = self.sbuf("mask_t", [P, P], BF16)
        self.mask = self.sbuf("mask", [P, P], BF16)
        self.sel = self.sbuf("sel", [P, 32], BF16)
        self.consts = {n: t for n, t in (
            ("ones", self.ones), ("ident", self.ident),
            ("ident16", self.ident16), ("mask_t", self.mask_t),
            ("mask", self.mask), ("sel", self.sel))}
        self.ssq = self.sbuf("ssq", [P, L])
        self.square = self.sbuf("square", [P, 2, L])
        self.mean = self.sbuf("mean", [P, L + 16])
        self.rinv = self.sbuf("rinv", [P, L + 16])
        self.scaled = self.sbuf("scaled", [P, 2, L])
        self.newton = self.sbuf("newton", [P, L + 16])
        self.psum = nc.alloc_psum_tensor("psum", [P, 8, 512], F32)

    def sbuf(self, name, shape, dt=F32, at=None):
        size = int(np.prod(shape[1:])) * (2 if dt == BF16 else 4)
        start = self.top if at is None else at
        if at is None:
            self.top += -(-size // 32) * 32
        return self.nc.alloc_sbuf_tensor_at("sb_" + name, shape, dt, offset=start)

    def sig(self, name):
        if name not in self.signals:
            self.signals[name] = self.nc.alloc_semaphore("s_" + name)
        return self.signals[name]

    def done(self, instr, name, by=1):
        instr.then_inc(self.sig(name), by)

    def ahead(self, name):
        return 0 if name in DMA_EVENTS else AHEAD + AHEAD_MORE.get(name, 0)

    def need(self, e, name, n):
        if not isinstance(n, int) or n > 0:
            e.wait_ge(self.sig(name), n + self.ahead(name))

    def head_start(self, e):
        for name in sorted(self.signals):
            if self.ahead(name):
                e.sem_inc(self.sig(name), self.ahead(name))

    def step(self, e, instr, name, n):
        self.done(instr, name)
        if name not in LATER:
            self.need(e, name, n)

    def col(self, name, i=0, rows=slice(0, P)):
        return self.cols[rows, bass.ds(COLS[name] + i, 1)]

    def both(self, bank):
        return self.psum[:, bank:bank + 2, 0:HALF]

    def load_weights(self, e):
        def load(u, k):
            self.done(e.dma_start(self.w_raw[:, k, :], self.ins["weights"][u]), f"load{k}", 16)

        for k in range(2):
            load(k, k)
        with e.Fori(1, UNITS // 2) as i:
            for k in range(2):
                self.need(e, "w_lo", 2 * i + k - 1)
                load(2 * i + k, k)
        for u in range(UNITS // 2 * 2, UNITS):
            self.need(e, "w_lo", u - 1)
            load(u, u % 2)

    def split_hi(self, e, u, k):
        slot, raw = k % 4, k % 2
        self.need(e, f"load{raw}", 8 * (u - raw) + 16)
        self.need(e, "unit", u - 3)
        self.step(e, e.activation(self.w_hi[:, slot, :], self.w_raw[:, raw, :], ACT.Copy), "w_hi", u + 1)

    def low(self, e, u, k):
        self.need(e, "w_hi", u + 1)
        self.step(e, e.tensor_tensor(self.w_lo[:, k % 4, :], self.w_raw[:, k % 2, :],
                                     self.w_hi[:, k % 4, :].bitcast(F32), ALU.subtract),
                  "w_lo", u + 1)

    def split_lo(self, e, first, last):
        whole = (last - first) // 4
        if whole:
            with e.Fori(0, whole) as i:
                for k in range(4):
                    self.low(e, 4 * i + (first + k), first + k)
        for u in range(first + 4 * whole, last):
            self.low(e, u, u)

    def unit(self, e, u, k, bank, x, width=None, plan=None, before=None, m=P):
        slot, (x_hi, x_lo, c0) = k % 4, x
        width = width or [HALF, HALF]
        plan = plan or [(i, i, bank, i == 0, i == 7) for i in range(8)]
        self.need(e, "w_lo", u + 1)
        for i, tile, at, first, last in plan:
            if before and i in before:
                for name, n in before[i]:
                    self.need(e, name, n)
            for n, (w, xs) in enumerate(((self.w_hi, x_hi), (self.w_hi, x_lo), (self.w_lo, x_hi))):
                c = c0
                for b, wd in enumerate(width):
                    mm = e.matmul(self.psum[0:m, at + b, 0:wd], w[:, slot, P * i:P * i + m],
                                  xs[:, tile, c:c + wd], start=first and n == 0,
                                  stop=last and n == 2)
                    c += wd
        self.done(mm, "unit")

    def rsqrt_act(self, e, n, width=L):
        self.ln_act(e, n, self.mean, self.rinv, width)
        self.exp_act(e, n, self.rinv, width)

    def ln_act(self, e, n, mean, rinv, width):
        self.need(e, "mean", n)
        self.step(e, e.activation(rinv[:, 0:width], mean[:, 0:width], ACT.Ln), "mean_ln", n)

    def exp_act(self, e, n, rinv, width):
        self.step(e, e.activation(rinv[:, 0:width], rinv[:, 0:width], ACT.Exp, scale=-0.5),
                  "rinv0", n)

    def rsqrt_dve(self, e, n, total, scale, width=L):
        self.mean_dve(e, n, total, scale, self.mean, width)
        self.newton_dve(e, n, self.mean, self.rinv, width)

    def mean_dve(self, e, n, total, scale, mean, width):
        mean = mean[:, 0:width]
        out = mean.rearrange("p (a b) -> p a b", a=2) if len(total.shape) == 3 else mean
        self.step(e, e.tensor_scalar(out, total, scale, EPS, ALU.mult, ALU.add), "mean", n)

    def newton_dve(self, e, n, mean, rinv, width):
        mean, y, t = mean[:, 0:width], rinv[:, 0:width], self.newton[:, 0:width]
        self.need(e, "rinv0", n)
        self.step(e, e.tensor_tensor(t, y, y, ALU.mult), "newton", 3 * n - 2)
        self.step(e, e.scalar_tensor_tensor(t, t, -0.5, mean, ALU.mult, ALU.mult), "newton",
                  3 * n - 1)
        self.step(e, e.scalar_tensor_tensor(y, t, 1.5, y, ALU.add, ALU.mult), "newton", 3 * n)

    def square_act(self, e, n, m, k):
        if isinstance(n, int) and n >= 3:
            self.need(e, "ssq", (n - 3) * KT + m - 1)
        elif m >= 2:
            self.need(e, "sq_sum", n * (KT - 1) + m - 1)
        self.step(e, e.activation(self.square[:, k, :], self.resid[:, m, :], ACT.Square), "sq", n * KT + m + 1)

    def ssq_dve(self, e, n, m, k):
        if isinstance(m, int) and m == KT - 1:
            return
        count = (n - 3) * KT + m
        self.need(e, "sq", n * KT + m + 1)
        self.need(e, "ssq", count)
        self.step(e, e.tensor_tensor(self.ssq[:, :], self.ssq[:, :], self.square[:, k, :], ALU.add),
                  "ssq", count + 1)

    def total_pe(self, e, name, parts, half=HALF):
        for n, (part, waits, event) in enumerate(parts):
            for w in waits:
                self.need(e, *w)
            for b in range(2):
                mm = e.matmul(self.psum[:, 6 + b, 0:half], self.ones[:, :],
                              part[:, half * b:half * b + half],
                              start=n == 0, stop=n == len(parts) - 1)
            if event:
                self.done(mm, event)
        self.done(mm, name)

    def norm_pe(self, e, n):
        if isinstance(n, int) and n >= 3:
            parts = [(self.ssq, [("ssq", (n - 3) * KT + KT - 1)], None),
                     (self.square[:, 1, :], [("sq", (n + 1) * KT)], None)]
        else:
            parts = [(self.square[:, m % 2, :], [("sq", n * KT + m + 1)],
                      "sq_sum" if m < KT - 1 else None) for m in range(KT)]
        self.total_pe(e, "norm_total", parts)

    def norm_act(self, e, n):
        self.rsqrt_act(e, rsqrt_norm(n))
        for k in range(KT):
            self.need(e, "h_scaled", n * KT + k + 1)
            self.step(e, e.activation(self.h_hi[:, k, :], self.normed(k), ACT.Copy),
                      "h_hi", n * KT + k + 1)

    def normed(self, k):
        return (self.scaled if k % 4 < 2 else self.square)[:, k % 2, :]

    def norm_low(self, e, n, k):
        self.need(e, "h_hi", n * KT + k + 1)
        event = self.h_low(n, k)
        self.done(e.tensor_tensor(self.h_lo[:, k, :], self.normed(k),
                                  self.h_hi[:, k, :].bitcast(F32), ALU.subtract), event[0])
        if k < KT - 2:
            self.need(e, *event)

    def h_low(self, n, k):
        return ("h_lo_odd" if k % 2 else "h_lo", n * (KT // 2) + k // 2 + 1)

    def norm_dve(self, e, n, gain):
        self.need(e, "norm_total", n + 1)
        self.rsqrt_dve(e, rsqrt_norm(n), self.both(6), 1.0 / D)
        for k in range(KT):
            if k >= 4:
                self.need(e, *self.h_low(n, k - 4))
            self.step(e, e.scalar_tensor_tensor(self.normed(k), self.resid[:, k, :],
                                             gain(k), self.rinv[:, 0:L], ALU.mult, ALU.mult),
                      "h_scaled", n * KT + k + 1)
            if k % 2:
                self.norm_low(e, n, k - 1)
        if isinstance(n, int) and 3 <= n < 5:
            self.step(e, e.memset(self.ssq[:, :], 0.0), "ssq", (n - 2) * KT)

    def norm_pool(self, e, n):
        for k in range(1, KT, 2):
            self.need(e, "h_scaled", n * KT + k + 1)
            self.norm_low(e, n, k)

    def h_ready(self, n):
        return {i: [self.h_low(n, i)] for i in range(KT)}


class Block1:

    T = slice(META, L)

    def __init__(self, b):
        self.b = b
        self.decay = b.sbuf("decay", [P, sum(WIDE1)])
        self.cos, self.sin = b.sbuf("cos", [P, SEQ]), b.sbuf("sin", [P, SEQ])
        self.q, self.k = b.sbuf("q", [P, SEQ]), b.sbuf("k", [P, SEQ])
        self.rot = b.sbuf("rot", [P, 2, SEQ])
        self.v_t, self.v = b.sbuf("v_t", [P, SEQ]), b.sbuf("v", [P, SEQ // P, P])
        self.s = b.sbuf("s", [P, sum(WIDE1)])
        self.c, self.u = b.sbuf("c", [P, SEQ]), b.sbuf("u", [P, 2 + SEQ])
        self.cz, self.rz = b.sbuf("cz", [P, SEQ]), b.sbuf("rz", [P, SEQ])
        self.y = b.sbuf("y", [P, 2, SEQ])

    def tables_act(self, e):
        b = self.b
        for n, t in enumerate((self.cos, self.sin)):
            b.need(e, "angle", n + 1)
            b.step(e, e.activation(t[:, :], t[:, :], ACT.Sin), "trig", n + 1)

    def tables_dve(self, e):
        b = self.b
        pos, ang, whole, red = self.v_t, self.q, self.k, self.s
        b.need(e, "pos", 16)
        b.need(e, "cols", 16)
        b.step(e, e.tensor_copy(pos[:, :], self.s[:, 0:SEQ].bitcast(I32)), "pos_f", 1)
        b.step(e, e.tensor_scalar(ang[:, :], pos[:, :], b.col("inv_freq"), None, ALU.mult),
               "ang", 1)
        for n, (table, turn) in enumerate(((self.cos, 0.25), (self.sin, 0.0))):
            s = 7 * n
            b.step(e, e.tensor_scalar(whole[:, :], ang[:, :], 1 / (2 * np.pi), turn, ALU.mult,
                                      ALU.add), "reduce", s + 1)
            b.step(e, e.tensor_scalar(whole[:, :], whole[:, :], ROUND, None, ALU.add),
                   "reduce", s + 2)
            b.step(e, e.tensor_scalar(whole[:, :], whole[:, :], ROUND, None, ALU.subtract),
                   "reduce", s + 3)
            b.step(e, e.scalar_tensor_tensor(red[:, 0:SEQ], whole[:, :], -TWO_PI[0], ang[:, :],
                                             ALU.mult, ALU.add), "reduce", s + 4)
            b.step(e, e.scalar_tensor_tensor(red[:, 0:SEQ], whole[:, :], -TWO_PI[1],
                                             red[:, 0:SEQ], ALU.mult, ALU.add), "reduce", s + 5)
            b.step(e, e.scalar_tensor_tensor(red[:, 0:SEQ], whole[:, :], -TWO_PI[2],
                                             red[:, 0:SEQ], ALU.mult, ALU.add), "reduce", s + 6)
            b.step(e, e.tensor_scalar(red[:, 0:SEQ], red[:, 0:SEQ], 2 * np.pi * turn, PI_BELOW,
                                      ALU.add, ALU.min), "reduce", s + 7)
            b.step(e, e.tensor_scalar(table[:, :], red[:, 0:SEQ], -PI_BELOW, None, ALU.max),
                   "angle", n + 1)
        b.need(e, "trig", 2)
        b.step(e, e.tensor_scalar(self.sin[:, :], self.sin[:, :], b.col("sin_sign"), None,
                                  ALU.mult), "signed", 1)
        b.step(e, e.memset(self.u[:, 0:2], 0.0), "u_pad", 1)

    def heads_pe(self, e, l, f):
        b, t = self.b, l * HEADS1 + f
        u = l * LAYER1 + f * ITER1
        x = (b.h_hi, b.h_lo, META)

        def unit(k, bank, before=None):
            b.unit(e, u + k, k, bank, x, [SEQ], before=before)

        b.need(e, "conv_x", t)
        unit(0, 0, b.h_ready(l))
        b.need(e, "conv_b", t)
        unit(1, 1)
        b.need(e, "cz", t)
        unit(2, 2)
        b.need(e, "rz", t)
        unit(3, 3)
        b.need(e, "v_t", t + 1)
        b.need(e, "mean", RSQRT_LAYER * l + f + 1)
        for j in range(SEQ // P):
            mm = e.transpose(b.psum[:, 7, P * j:P * j + P], self.v_t[:, P * j:P * j + P],
                             b.ident[:, :])
        b.done(mm, "v_turned")
        b.need(e, "q_read", t + 1)
        unit(4, 0)
        b.need(e, "k_rot", t + 1)
        for j in range(SEQ // P):
            if j == 2:
                b.need(e, "k_read", t + 1)
                unit(5, 1)
            b.need(e, "decayed", 4 * t + j - 1)
            mm = e.matmul(b.psum[:, 4 + j % 2, 0:WIDE1[j]], self.k[:, P * j:P * j + P],
                          self.q[:, P * j:SEQ], start=True, stop=True)
            b.done(mm, "scores")
        unit(6, 2)
        b.need(e, "v", t + 1)
        b.need(e, "ret_y", t)
        for j in range(SEQ // P):
            b.need(e, "decayed", 4 * t + j + 1)
            mm = e.matmul(b.psum[:, 6, P * j:SEQ], self.v[:, j, :],
                          self.s[:, OFF1[j]:OFF1[j] + WIDE1[j]], start=j == 0, stop=j == 3)
        b.done(mm, "ret")
        b.need(e, "c", t + 1)
        unit(7, 3)
        b.need(e, "ret_sq", t + 1)
        b.done(e.matmul(b.psum[:, 7, :], b.ones[:, :], b.square[:, 0, 0:SEQ], start=True,
                        stop=True), "ret_total")

    def heads_act(self, e, l, f):
        b, t = self.b, l * HEADS1 + f
        u = l * LAYER1 + f * ITER1

        def split(k):
            b.split_hi(e, u + k + LEAD, k + LEAD)

        def result(k):
            split(k)
            b.need(e, "unit", u + k + 1)

        b.need(e, "decayed", 4 * t)
        b.done(e.dma_start(self.decay[:, :], b.ins["decay"][f]), "decay", 16)
        split(0)
        split(1)
        result(2)
        b.step(e, e.activation(self.v_t[:, :], b.psum[:, 2, :], ACT.Copy), "v_t", t + 1)
        result(3)
        b.step(e, e.activation(self.c[:, :], b.psum[:, 3, :], ACT.Copy), "c", t + 1)
        b.need(e, "v_turned", t + 1)
        b.step(e, e.activation(self.v[:, :, :], b.psum[:, 7, :], ACT.Copy), "v", t + 1)
        split(4)
        split(5)
        result(6)
        b.step(e, e.activation(self.cz[:, :], b.psum[:, 2, :], ACT.Silu), "cz", t + 1)
        b.need(e, "conv_y", t + 1)
        b.step(e, e.activation(b.mix_hi[:, f, self.T], self.y[:, 0, :], ACT.Copy), "mix_hi", 2 * t + 1)
        split(7)
        b.need(e, "ret", t + 1)
        b.step(e, e.activation(b.square[:, 0, 0:SEQ], b.psum[:, 6, :], ACT.Square), "ret_sq", t + 1)
        b.need(e, "unit", u + 8)
        b.step(e, e.activation(self.rz[:, :], b.psum[:, 3, :], ACT.Silu), "rz", t + 1)
        b.rsqrt_act(e, RSQRT_LAYER * l + f + 2, SEQ)
        b.need(e, "mix_y", t + 1)
        b.step(e, e.activation(b.mix_hi[:, KT + f, self.T], self.y[:, 1, :], ACT.Copy), "mix_hi", 2 * t + 2)

    def rotate(self, e, bank, out, read, final, n):
        b = self.b
        half = P // 2
        for lo, hi in ((0, half), (half, 0)):
            b.step(e, e.tensor_tensor(self.rot[lo:lo + half, 0, :], b.psum[hi:hi + half, bank, :],
                                   self.sin[hi:hi + half, :], ALU.mult), read + "_part", 2 * n - 1 + lo // half)
        b.step(e, e.tensor_tensor(self.rot[:, 1, :], b.psum[:, bank, :], self.cos[:, :],
                                  ALU.mult), read, n)
        b.need(e, read + "_part", 2 * n)
        b.step(e, e.tensor_tensor(out[:, :], self.rot[:, 0, :], self.rot[:, 1, :], ALU.add), final, n)

    def low(self, e, tile, y, n):
        b = self.b
        b.need(e, "mix_hi", n)
        b.step(e, e.tensor_tensor(b.mix_lo[:, tile, self.T], y,
                               b.mix_hi[:, tile, self.T].bitcast(F32), ALU.subtract), "mix", n)

    def heads_dve(self, e, l, f):
        b, t = self.b, l * HEADS1 + f
        u = l * LAYER1 + f * ITER1
        b.need(e, "unit", u + 1)
        self.rotate(e, 0, self.q, "q_read", "q_rot", t + 1)
        b.need(e, "unit", u + 2)
        self.rotate(e, 1, self.k, "k_read", "k_rot", t + 1)
        b.need(e, "unit", u + 5)
        b.need(e, "c", t + 1)
        b.step(e, e.tensor_tensor(self.u[:, 2:2 + SEQ], b.psum[:, 0, :], self.c[:, :], ALU.mult),
               "conv_x", t + 1)
        tap = lambda j: b.col("conv", l * (3 * KT) + f * 3 + j)
        conv = self.y[:, 0, :]
        b.step(e, e.tensor_scalar(conv, self.u[:, 2:2 + SEQ], tap(2), None, ALU.mult),
               "tap2", t + 1)
        b.step(e, e.scalar_tensor_tensor(conv, self.u[:, 1:1 + SEQ], tap(1), conv, ALU.mult,
                                         ALU.add), "tap1", t + 1)
        b.step(e, e.scalar_tensor_tensor(conv, self.u[:, 0:SEQ], tap(0), conv, ALU.mult,
                                         ALU.add), "tap0", t + 1)
        b.need(e, "decay", 16 * (t + 1))

        def decayed(j):
            b.need(e, "scores", 4 * t + j + 1)
            at = slice(OFF1[j], OFF1[j] + WIDE1[j])
            b.step(e, e.tensor_tensor(self.s[:, at], b.psum[:, 4 + j % 2, 0:WIDE1[j]],
                                   self.decay[:, at], ALU.mult), "decayed", 4 * t + j + 1)

        decayed(0)
        decayed(1)
        b.need(e, "unit", u + 6)
        b.step(e, e.tensor_tensor(conv, b.psum[:, 1, :], conv, ALU.mult), "conv_b", t + 1)
        decayed(2)
        decayed(3)
        b.need(e, "conv_b", t + 1)
        b.need(e, "cz", t + 1)
        b.step(e, e.tensor_tensor(conv, conv, self.cz[:, :], ALU.mult), "conv_y", t + 1)
        self.low(e, f, conv, 2 * t + 1)
        b.need(e, "ret_total", t + 1)
        b.rsqrt_dve(e, RSQRT_LAYER * l + f + 2, b.psum[:, 7, :], 1.0 / P, SEQ)
        y = self.y[:, 1, :]
        b.step(e, e.tensor_tensor(y, b.psum[:, 6, :], b.rinv[:, 0:SEQ], ALU.mult), "ret_y", t + 1)
        b.need(e, "rz", t + 1)
        b.step(e, e.tensor_tensor(y, y, self.rz[:, :], ALU.mult), "mix_y", t + 1)
        self.low(e, KT + f, y, 2 * t + 2)

    def out_pe(self, e, l, i):
        b = self.b
        for j in range(2):
            m, k = 2 * i + j, 2 * j
            u = l * LAYER1 + HEADS1 * ITER1 + 4 * i + k
            x = (b.mix_hi, b.mix_lo, META)
            b.need(e, "o_sq", l * KT + m - 1)
            b.unit(e, u, k, j, x, [SEQ], [(n, n, j, n == 0, False) for n in range(8)],
                   {0: [("mix", 16 * l + 15)]})
            b.unit(e, u + 1, k + 1, j, x, [SEQ], [(n, 8 + n, j, False, n == 7) for n in range(8)],
                   {7: [("mix", 16 * l + 16)]})

    def out_act(self, e, l, i):
        b = self.b
        for j in range(2):
            m, k = 2 * i + j, 2 * j
            u = l * LAYER1 + HEADS1 * ITER1 + 4 * i + k
            b.split_hi(e, u + LEAD, k + LEAD)
            b.split_hi(e, u + 1 + LEAD, k + 1 + LEAD)
            b.need(e, "unit", u + 2)
            b.step(e, e.activation(b.o[:, m, :], b.psum[:, j, :], ACT.Copy), "o", l * KT + m + 1)
            b.need(e, "ossq", l * KT + m - 1)
            b.step(e, e.activation(b.square[:, j, 0:SEQ], b.psum[:, j, :], ACT.Square), "o_sq",
                   l * KT + m + 1)

    def out_dve(self, e, l):
        b = self.b
        with e.Fori(0, KT // 2 - 1) as i:
            for j in range(2):
                self.ossq(e, l, 2 * i + j, j)
        self.ossq(e, l, KT - 2, 0)

    def ossq(self, e, l, m, j):
        b = self.b
        b.need(e, "o_sq", l * KT + m + 1)
        b.need(e, "ossq", l * KT + m)
        b.step(e, e.tensor_tensor(b.ssq[:, 0:SEQ], b.ssq[:, 0:SEQ], b.square[:, j, 0:SEQ],
                                  ALU.add), "ossq", l * KT + m + 1)

    def post_pe(self, e, l):
        b = self.b
        b.total_pe(e, "post_total", [
            (b.ssq, [("ossq", (l + 1) * KT - 1)], None),
            (b.square[:, 1, :], [("o_sq", (l + 1) * KT)], None)], SEQ // 2)

    def post_act(self, e, l):
        b = self.b
        b.rsqrt_act(e, RSQRT_LAYER * (l + 1), SEQ)
        for m in range(KT):
            b.need(e, *self.resid_done(l, m))
            b.square_act(e, l + 1, m, m % 2)

    def resid_done(self, l, m):
        return ("resid_odd" if m % 2 else "resid", l * (KT // 2) + m // 2 + 1)

    def post_slot(self, m):
        return (self.decay, self.s)[m % 2][:, SEQ * (m // 2 % 2):SEQ * (m // 2 % 2) + SEQ]

    def post_add(self, e, l, m):
        b = self.b
        b.need(e, "post_o", l * KT + m + 1)
        b.step(e, e.tensor_tensor(b.resid[:, m, self.T], b.resid[:, m, self.T],
                                  self.post_slot(m), ALU.add), *self.resid_done(l, m))

    def post_dve(self, e, l):
        b = self.b
        b.need(e, "post_total", l + 1)
        b.rsqrt_dve(e, RSQRT_LAYER * (l + 1), b.psum[:, 6:8, 0:SEQ // 2], 1.0 / D, SEQ)
        b.step(e, e.memset(b.ssq[:, :], 0.0), "ossq", (l + 1) * KT)
        for m in range(KT):
            if m >= 4:
                b.need(e, *self.resid_done(l, m - 4))
            b.step(e, e.scalar_tensor_tensor(self.post_slot(m), b.o[:, m, :],
                                             b.col("post", l * KT + m), b.rinv[:, 0:SEQ],
                                             ALU.mult, ALU.mult), "post_o", l * KT + m + 1)
            if m % 2 == 0:
                self.post_add(e, l, m)

    def post_pool(self, e, l):
        for m in range(1, KT, 2):
            self.post_add(e, l, m)


class Adds:

    SSD, MLP0, MLA, MLP1 = 0, KT, KT + QUARTERS * KT, 2 * KT + QUARTERS * KT

    def __init__(self, b):
        self.b = b

    def act(self, e, count, m, k, norm):
        if norm is not None:
            self.b.need(e, "add", count + m + 1)
            self.b.square_act(e, norm, m, k % 2)

    def dve(self, e, count, m, k, units_done, norm):
        b = self.b
        b.need(e, "unit", units_done)
        r = b.resid[:, m, :].rearrange("p (a c) -> p a c", a=2)
        b.step(e, e.tensor_tensor(r, r, b.both(2 * (k % 2)), ALU.add), "add", count + m + 1)
        if norm is not None:
            b.ssq_dve(e, norm, m, k % 2)


    def all_dve(self, e, count, units_done, norm):
        with e.Fori(0, KT // 2 - 1) as i:
            for j in range(2):
                self.dve(e, count, 2 * i + j, j, units_done(2 * i + j), norm)
        for m in range(KT - 2, KT):
            self.dve(e, count, m, m, units_done(m), norm)


class Mlp:

    def __init__(self, b, adds, units, norm, next_norm, first_quarter, count):
        self.b, self.adds, self.units, self.norm = b, adds, units, norm
        self.next_norm = next_norm
        self.q0, self.count = first_quarter, count

    def up_pe(self, e, qi, i):
        b, q = self.b, self.q0 + qi
        for j in range(4):
            m, u = 4 * i + j, self.units + 2 * KT * qi + 4 * i + j
            b.need(e, "relu", q * KT + m - 1)
            b.need(e, "add", self.count + qi * KT - 1 + min(j, 1))
            b.unit(e, u, 1 + j, 2 * (j % 2), (b.h_hi, b.h_lo, 0),
                   before=b.h_ready(self.norm) if j == 0 else None)

    def down_pe(self, e, qi, i, final):
        b, q = self.b, self.q0 + qi
        for j in range(4):
            m, u = 4 * i + j, self.units + 2 * KT * qi + KT + 4 * i + j
            b.need(e, "relu", (q + 1) * KT - 1 + min(j, 1))
            b.need(e, "add", self.count + qi * KT + m - 1)
            b.unit(e, u, 1 + j, 2 * (j % 2), (b.mix_hi, b.mix_lo, 0),
                   before={n: [("hidden", q * KT + n + 1)] for n in range(KT)} if j == 0 else None)

    def up_act(self, e, qi, i):
        b, q = self.b, self.q0 + qi
        for j in range(4):
            m, u = 4 * i + j, self.units + 2 * KT * qi + 4 * i + j
            n = q * KT + m + 1
            b.split_hi(e, u + LEAD, 1 + j + LEAD)
            b.need(e, "unit", u + 1)
            t = b.square[:, j % 2, :].rearrange("p (a c) -> p a c", a=2)
            b.step(e, e.activation(t, b.both(2 * (j % 2)), ACT.Relu), "relu", n)
            b.need(e, "relu_sq", n)
            b.step(e, e.activation(b.mix_hi[:, m, :], b.scaled[:, j % 2, :], ACT.Copy),
                   "hidden_hi", n)

    def down_act(self, e, qi, i, final):
        b = self.b
        norm = self.next_norm if final else None
        for j in range(4):
            u = self.units + 2 * KT * qi + KT + 4 * i + j
            if not (final and self.units == U_MLP1 and 4 * i + j + LEAD >= KT):
                b.split_hi(e, u + LEAD, 1 + j + LEAD)
            self.adds.act(e, self.count + qi * KT, 4 * i + j, j, norm)

    def up_dve(self, e, qi, i):
        b, q = self.b, self.q0 + qi
        for j in range(4):
            m = 4 * i + j
            n = q * KT + m + 1
            t = b.square[:, j % 2, :]
            b.need(e, "relu", n)
            b.step(e, e.tensor_tensor(b.scaled[:, j % 2, :], t, t, ALU.mult), "relu_sq", n)
            b.need(e, "hidden_hi", n)
            b.step(e, e.tensor_tensor(b.mix_lo[:, m, :], b.scaled[:, j % 2, :],
                                      b.mix_hi[:, m, :].bitcast(F32), ALU.subtract), "hidden", n)

    def down_dve(self, e, qi, i, final):
        norm = self.next_norm if final else None
        for j in range(4):
            u = self.units + 2 * KT * qi + KT + 4 * i + j
            self.adds.dve(e, self.count + qi * KT, 4 * i + j, j, u + 1, norm)

    def run(self, e, up, down):
        with e.Fori(0, QUARTERS - 1) as qi:
            with e.Fori(0, 2) as i:
                up(e, qi, i)
            with e.Fori(0, 2) as i:
                down(e, qi, i, False)
        with e.Fori(0, 2) as i:
            up(e, QUARTERS - 1, i)
        for i in range(2):
            down(e, QUARTERS - 1, i, True)


class Ssd:

    PIECES = [(0, 0, HALF), (0, HALF, HALF)] + [(j, P * j, WIDE[j]) for j in range(1, NT)]
    NP = len(PIECES)
    SLOTS = 4
    BANKS = (6, 7, 0, 1)
    HG = 4

    def __init__(self, b):
        self.b = b
        self.cb = b.sbuf("cb", [P, CAUSAL])
        self.rest = b.sbuf("rest", [P, CAUSAL], at=b.top)
        self.part = b.sbuf("part", [P, self.SLOTS, max(w for _, _, w in self.PIECES[2:])])
        self.xdt = b.sbuf("xdt", [P, NT, self.HG * 64])
        self.bt, self.ct = b.sbuf("bt", [P, L]), b.sbuf("ct", [P, L])
        self.x, self.z = b.sbuf("x", [P, 2, L]), b.sbuf("z", [P, 2, L])
        self.y = b.sbuf("y2", [P, 2, L])
        self.lift = b.sbuf("lift", [P, 2, 3 + L])
        self.rows = b.sbuf("rows", [P, CAUSAL], BF16)
        self.dt_tok, self.neg_a = b.sbuf("dt_tok", [P, NT, 32]), b.sbuf("neg_a", [P, NT, 32])
        self.a = b.sbuf("a", [P, 1])
        self.bias = b.sbuf("bias", [P, NT, self.HG])

    def dt_pe(self, e):
        b = self.b
        b.unit(e, U_DT, 0, 4, (b.h_hi, b.h_lo, 0), before=b.h_ready(2))

    def dt_turn(self, e):
        b = self.b
        b.need(e, "dt_v", self.DT_SUMS)
        for j, w in enumerate(TILES):
            e.transpose(b.psum[0:w, 6, 32 * j:32 * j + 32], b.square[0:32, 0, P * j:P * j + w],
                        b.ident[0:32, 0:32])
        for j, w in enumerate(TILES):
            mm = e.transpose(b.psum[0:w, 7, 32 * j:32 * j + 32],
                             self.cb[0:32, OFF[j]:OFF[j] + w], b.ident[0:32, 0:32])
        b.done(mm, "dt_turned")

    def dt_act(self, e):
        b = self.b
        b.split_hi(e, U_DT + LEAD, LEAD)
        b.step(e, e.activation(self.a[:, :], b.col("a_log"), ACT.Exp), "dt_a", 1)
        b.need(e, "dt_v", 4)
        b.step(e, e.activation(self.x[:, 1, :], self.x[:, 0, :], ACT.Exp), "dt_a", 2)
        b.need(e, "dt_v", 5)
        b.step(e, e.activation(self.y[:, 0, :], self.z[:, 0, :], ACT.Ln), "dt_a", 3)

    DT_SUMS = 22 + NT

    def dt_dve(self, e):
        b = self.b
        count = [0]

        def do(instr):
            count[0] += 1
            b.step(e, instr, "dt_v", count[0])

        v, dt, ex = self.bt[:, :], b.square[:, 0, :], self.x[:, 1, :]
        w, d, ln, eq = self.z[:, 0, :], self.z[:, 1, :], self.y[:, 0, :], self.y[:, 1, :]
        b.need(e, "unit", U_DT + 1)
        do(e.memset(self.lift[:, :, 0:3], 0.0))
        do(e.tensor_scalar(halves(v), b.both(4), b.col("dt_bias"), None, ALU.add))
        do(e.tensor_scalar(dt, v, 0.0, None, ALU.max))
        do(e.scalar_tensor_tensor(self.x[:, 0, :], dt, -2.0, v, ALU.mult, ALU.add))
        b.need(e, "dt_a", 2)
        do(e.tensor_scalar(w, ex, 1.0, None, ALU.add))
        do(e.tensor_scalar(d, w, 1.0, None, ALU.subtract))
        do(e.tensor_scalar(eq, d, 0.0, None, ALU.is_equal))
        do(e.tensor_tensor(d, d, eq, ALU.add))
        do(e.reciprocal(v, d))
        b.need(e, "dt_a", 3)
        do(e.tensor_tensor(ln, ln, v, ALU.mult))
        do(e.tensor_tensor(ln, ln, eq, ALU.add))
        do(e.tensor_tensor(ln, ln, ex, ALU.mult))
        do(e.tensor_tensor(dt, dt, ln, ALU.add))
        do(e.tensor_scalar(self.a[:, :], self.a[:, :], -1.0, None, ALU.mult))
        do(e.tensor_scalar(v, dt, self.a[:, 0:1], None, ALU.mult))
        do(e.memset(self.x[:, 0, :], 1.0))
        for j, wd in enumerate(WIDE):
            do(e.tensor_tensor_scan(self.cb[:, OFF[j]:OFF[j] + wd], self.x[:, 0, 0:wd],
                                    v[:, P * j:L], 0.0, ALU.mult, ALU.add))
        rest, rows, sums = self.rest, self.rows, self.cb
        do(e.tensor_copy(rows[:, :], sums[:, :]))
        do(e.tensor_tensor(rest[:, :], sums[:, :], rows[:, :], ALU.subtract))
        do(e.tensor_copy(rows[32:64, :], rest[32:64, :]))
        do(e.tensor_copy(rows[64:96, :], rest[64:96, :]))
        do(e.tensor_tensor(rest[64:96, :], rest[64:96, :], rows[64:96, :], ALU.subtract))
        do(e.tensor_copy(rows[64:96, :], rest[64:96, :]))
        assert count[0] == self.DT_SUMS

    def dt_tokens(self, e):
        b = self.b
        count = self.DT_SUMS
        b.need(e, "dt_turned", 1)
        for out, bank, s in ((self.dt_tok, 6, 1.0), (self.neg_a, 7, -1.0)):
            for rows_, tiles in ((P, slice(0, NT - 1)), (TILES[-1], slice(NT - 1, NT))):
                src = b.psum[0:rows_, bank, 0:32 * NT].rearrange("p (j h) -> p j h", h=32)
                count += 1
                b.step(e, e.tensor_scalar(out[0:rows_, tiles, :], src[:, tiles, :], s, None,
                                          ALU.mult), "dt_v", count)

    DT_ALL = DT_SUMS + 4

    def project_pe(self, e, g, s, units):
        b = self.b
        u = U_SSD + GROUP * g
        for k in units:
            if k < 2:
                b.need(e, "z2", 2 * g + k - 1)
            else:
                b.need(e, "lifted", 4 * g + k - 1)
            b.unit(e, u + k, s + k, 2 * (k % 2), (b.h_hi, b.h_lo, 0))

    def group_pe(self, e, g, s, last=False):
        b = self.b
        NP = self.NP
        b.need(e, "silu", 4 * g + 2)
        b.need(e, "mean", RSQRT_GROUPS + g)
        b.need(e, "dt_v", self.DT_ALL)
        for p, (j, l0, w) in enumerate(self.PIECES):
            b.need(e, "cb", NP * g + p - 1)
            b.done(e.matmul(b.psum[0:TILES[j], 6 + p % 2, 0:w],
                            self.bt[:, P * j:P * j + TILES[j]], self.ct[:, l0:l0 + w],
                            start=True, stop=True), "cb_sum")
        b.need(e, "silu", 4 * g + 4)
        b.need(e, "cb", NP * g + NP)
        b.need(e, "skip", 2 * g)
        for c in range(2):
            for j in range(NT - 1):
                mm = e.transpose(b.psum[:, 6 + c, P * j:P * j + P], self.x[:, c, P * j:P * j + P],
                                 b.ident[:, :])
            b.done(mm, "x_turned")
        for c in range(2):
            mm = e.transpose(b.psum[0:TILES[-1], 4, P * c:P * c + P], self.x[:, c, P * (NT - 1):L],
                             b.ident[:, :])
        b.done(mm, "x_turned")
        total = self.HG * NP

        def sums(n):
            h, p = divmod(n, NP)
            j, l0, w = self.PIECES[p]
            r = TILES[j]
            if n < 2:
                b.need(e, "xdt", 3 * g + n + 1)
            if n == 2:
                b.need(e, "z2", 2 * g + 2)
            b.need(e, "decay2", total * g + n + 1 - self.SLOTS)
            at = OFF[j] + l0 - P * j
            diagonal = l0 == P * j
            mm = e.matmul(b.psum[:, self.BANKS[n % 4], 0:w],
                          b.sel[0:96, bass.ds(self.HG * g + h, 1)].to_broadcast([96, P]),
                          self.rows[0:96, at:at + w], start=True, stop=not diagonal)
            if diagonal:
                mm = e.matmul(b.psum[:, self.BANKS[n % 4], 0:r], b.ident16[:, :], b.mask_t[:, 0:r],
                              start=False, stop=True)
            b.done(mm, "a_row")

        def y(n):
            h, p = divmod(n, NP)
            j, l0, w = self.PIECES[p]
            r, row = TILES[j], 64 * (h % 2)
            if p == 0 and h % 2 == 0:
                b.need(e, "skip", 2 * g + h // 2)
                b.need(e, "xdt", 3 * g + 3)
            b.need(e, "weighted", total * g + n + 1)
            for half in range(2):
                lo, hi = max(l0, HALF * half), min(l0 + w, HALF * (half + 1))
                if lo < hi:
                    mm = e.matmul(b.psum[row:row + 64, 4 + half, lo - HALF * half:hi - HALF * half],
                                  self.xdt[0:r, j, 64 * h:64 * h + 64],
                                  self.part[0:r, n % self.SLOTS, lo - l0:hi - l0],
                                  start=p == half, stop=p == (3 if half == 0 else NP - 1))
            b.done(mm, "y_part")

        ahead = self.SLOTS - 1
        for n in range(total + ahead):
            if n < total:
                sums(n)
            if n >= ahead:
                y(n - ahead)
        b.need(e, "decay2", total * (g + 1))
        if not last:
            self.project_pe(e, g + 1, s + GROUP, range(1))
        for c in range(2):
            b.need(e, "y_sq", 2 * g + c + 1)
            for half in range(2):
                mm = e.matmul(b.psum[:, 6 + half, 0:HALF], b.ones[:, :],
                              b.square[:, c, HALF * half:HALF * half + HALF],
                              start=c == 0, stop=c == 1)
        b.done(mm, "group_total")
        if not last:
            self.project_pe(e, g + 1, s + GROUP, range(1, GROUP))

    def silu_act(self, e, g, k):
        b = self.b
        out = (self.bt[:, :], self.ct[:, :], self.x[:, 0, :], self.x[:, 1, :])[k]
        b.need(e, "conv2", 4 * g + k + 1)
        b.step(e, e.activation(out, b.scaled[:, k % 2, :], ACT.Silu), "silu", 4 * g + k + 1)

    def project_act(self, e, g, s, units):
        b = self.b
        for k in units:
            u = U_SSD + GROUP * g + k
            b.split_hi(e, u + LEAD, s + k + LEAD)
            b.need(e, "unit", u + 1)
            if k == 2:
                self.silu_act(e, g, 0)
            if k < 4:
                b.step(e, e.activation(halves(self.lift[:, k % 2, 3:3 + L]), b.both(2 * (k % 2)),
                                       ACT.Copy), "lifted", 4 * g + k + 1)
            else:
                b.step(e, e.activation(halves(self.z[:, k - 4, :]), b.both(2 * (k % 2)),
                                       ACT.Silu), "z2", 2 * g + k - 3)
            if 2 <= k <= 4:
                self.silu_act(e, g, k - 1)

    def group_act(self, e, g, s, last=False):
        b = self.b
        NP = self.NP
        total = self.HG * NP
        for p, (j, l0, w) in enumerate(self.PIECES):
            r, at = TILES[j], OFF[j] + l0 - P * j
            b.need(e, "cb_sum", NP * g + p + 1)
            b.step(e, e.activation(self.cb[0:r, at:at + w], b.psum[0:r, 6 + p % 2, 0:w],
                                   ACT.Copy), "cb", NP * g + p + 1)

        def square(c):
            b.need(e, "gated", 2 * g + c + 1)
            b.step(e, e.activation(b.square[:, c, :], self.y[:, c, :], ACT.Square), "y_sq",
                   2 * g + c + 1)

        b.need(e, "bias", 2 * g + 2)
        for n in range(total):
            h, p = divmod(n, NP)
            j, _, w = self.PIECES[p]
            r = TILES[j]
            b.need(e, "a_row", total * g + n + 1)
            b.need(e, "y_part", total * g + n + 1 - self.SLOTS)
            b.done(e.activation(self.part[0:r, n % self.SLOTS, 0:w],
                                b.psum[0:r, self.BANKS[n % 4], 0:w], ACT.Exp,
                                bias=self.bias[0:r, j, h:h + 1]), "decay2")
            if n == 2 * NP + 3:
                square(0)
        square(1)
        if not last:
            self.project_act(e, g + 1, s + GROUP, range(1))
        b.rsqrt_act(e, RSQRT_GROUPS + g + 1)
        if not last:
            self.project_act(e, g + 1, s + GROUP, range(1, 2))
        for c in range(2):
            b.need(e, "group_y", 2 * g + c + 1)
            b.step(e, e.activation(b.mix_hi[:, 2 * g + c, :], self.y[:, c, :], ACT.Copy),
                   "mix2_hi", 2 * g + c + 1)
        if not last:
            self.project_act(e, g + 1, s + GROUP, range(2, GROUP))

    def project_dve(self, e, g, units):
        b = self.b
        for k in units:
            ch = (16 + g, 24 + g, 2 * g, 2 * g + 1)[k]
            out, n = b.scaled[:, k % 2, :], 4 * g + k + 1
            tap = lambda t: (self.lift[:, k % 2, t:t + L], b.col("ssd_conv", 4 * ch + t))
            b.need(e, "silu", n - 2)
            b.need(e, "lifted", n)
            x3, w3 = tap(3)
            b.step(e, e.tensor_scalar(out, x3, w3, b.col("ssd_bias", ch), ALU.mult, ALU.add),
                   "tap", 3 * n - 2)
            for t in (2, 1, 0):
                xt, wt = tap(t)
                b.step(e, e.scalar_tensor_tensor(out, xt, wt, out, ALU.mult, ALU.add),
                       *(("tap", 3 * n - t + 1) if t else ("conv2", n)))

    def group_dve(self, e, g, s, last=False):
        b = self.b
        NP = self.NP
        total = self.HG * NP
        tail = TILES[-1]
        for n, (w, t) in enumerate(((P, slice(0, NT - 1)), (tail, slice(NT - 1, NT)))):
            b.step(e, e.tensor_copy(self.bias[0:w, t, :],
                                    self.neg_a[0:w, t, bass.ds(self.HG * g, self.HG)]),
                   "bias", 2 * g + n + 1)
        for c in range(2):
            b.need(e, "x_turned", 3 * g + c + 1)
            ps = b.psum[:, 6 + c, :].rearrange("p (j h d) -> p j h d", j=NT - 1, h=2)
            dt = self.dt_tok[:, 0:NT - 1, bass.ds(self.HG * g + 2 * c, 2)]
            out = self.xdt[:, 0:NT - 1, P * c:P * c + P].rearrange("p j (h d) -> p j h d", h=2)
            b.step(e, e.tensor_tensor(out, ps, dt.unsqueeze(3).to_broadcast([P, NT - 1, 2, 64]),
                                      ALU.mult), "xdt", 3 * g + c + 1)
        b.need(e, "x_turned", 3 * g + 3)
        dt = self.dt_tok[0:tail, NT - 1, bass.ds(self.HG * g, self.HG)]
        b.step(e, e.tensor_tensor(
            self.xdt[0:tail, NT - 1, :].rearrange("p (h d) -> p h d", d=64),
            b.psum[0:tail, 4, 0:64 * self.HG].rearrange("p (h d) -> p h d", d=64),
            dt.unsqueeze(2).to_broadcast([tail, self.HG, 64]), ALU.mult), "xdt", 3 * g + 3)

        def finish(c):
            b.need(e, "y_part", total * g + 2 * NP * (c + 1))
            y = self.y[:, c, :]
            b.step(e, e.scalar_tensor_tensor(halves(y), halves(self.x[:, c, :]),
                                             b.col("ssd_d", 2 * g + c), b.both(4), ALU.mult,
                                             ALU.add), "skip", 2 * g + c + 1)
            b.step(e, e.tensor_tensor(y, y, self.z[:, c, :], ALU.mult), "gated", 2 * g + c + 1)

        for n in range(total):
            h, p = divmod(n, NP)
            j, l0, w = self.PIECES[p]
            r, at = TILES[j], OFF[j] + l0 - P * j
            part = self.part[0:r, n % self.SLOTS, 0:w]
            b.need(e, "decay2", total * g + n + 1)
            if n == 0:
                b.need(e, "cb", NP * (g + 1))
            b.done(e.tensor_tensor(part, part, self.cb[0:r, at:at + w], ALU.mult), "weighted")
            if n == 2 * NP + 1:
                finish(0)
        finish(1)
        if not last:
            self.project_dve(e, g + 1, range(1))
        b.need(e, "group_total", g + 1)
        b.rsqrt_dve(e, RSQRT_GROUPS + g + 1, b.both(6), 1.0 / 256)
        for c in range(2):
            y, n = self.y[:, c, :], 2 * g + c + 1
            b.step(e, e.scalar_tensor_tensor(y, y, b.col("ssd_norm", 2 * g + c), b.rinv[:, 0:L],
                                             ALU.mult, ALU.mult), "group_y", n)
        for c in range(2):
            n = 2 * g + c + 1
            b.need(e, "mix2_hi", n)
            b.step(e, e.tensor_tensor(b.mix_lo[:, 2 * g + c, :], self.y[:, c, :],
                                      b.mix_hi[:, 2 * g + c, :].bitcast(F32), ALU.subtract),
                   "mix2", n)
        if not last:
            self.project_dve(e, g + 1, range(1, 4))

    def run(self, e, group):
        with e.Fori(0, GROUPS // 2 - 1) as i:
            for j in range(2):
                group(e, 2 * i + j, 1 + GROUP * j)
        group(e, GROUPS - 2, 1)
        group(e, GROUPS - 1, 1 + GROUP, last=True)

    def out_pe(self, e, i):
        b = self.b
        for j in range(2):
            m, u = 2 * i + j, U_SSD_OUT + 4 * i + 2 * j
            x = (b.mix_hi, b.mix_lo, 0)
            bank = 2 * j
            b.need(e, "z2", 2 * GROUPS)
            b.need(e, "add", Adds.SSD + m - 1)
            b.unit(e, u, 1 + 2 * j, bank, x, None, [(n, n, bank, n == 0, False) for n in range(8)])
            b.unit(e, u + 1, 2 + 2 * j, bank, x, None,
                   [(n, 8 + n, bank, False, n == 7) for n in range(8)],
                   {n: [("mix2", 9 + n)] for n in range(8)})

    def out_act(self, e, adds, i):
        for j in range(2):
            u = U_SSD_OUT + 4 * i + 2 * j
            self.b.split_hi(e, u + LEAD, 1 + 2 * j + LEAD)
            self.b.split_hi(e, u + 1 + LEAD, 2 + 2 * j + LEAD)
            adds.act(e, Adds.SSD, 2 * i + j, j, 3)

    def out_dve(self, e, adds):
        adds.all_dve(e, Adds.SSD, lambda m: U_SSD_OUT + 2 * m + 2, 3)


class Mla:

    STEPS = [(h, t) for h in range(2) for t in range(NT)]
    Q_COLS = -(-NT // 2)
    WIDTH = L + 2 * Q_COLS

    def __init__(self, b):
        self.b = b
        self.v = b.sbuf("v_all", [P, NT, 2 * PAIRS * 64])
        self.lat = b.sbuf("lat", [P, 5, L], at=b.top)
        self.q, self.k = b.sbuf("q2", [P, 2, L]), b.sbuf("k2", [P, 2, L])
        self.p = b.sbuf("p", [P, 2, L])
        self.kpe, self.ksq = b.sbuf("kpe", [P, L]), b.sbuf("ksq", [P, 2, L])
        self.table = b.sbuf("table", [P, L])
        self.pt = b.sbuf("pt", [P, 2, 512])
        self.out = b.sbuf("out2", [P, NT, P])
        self.v2 = b.sbuf("v_pair", [P, NT, P], at=b.base)
        at = [b.h_lo_at + 4 * (L + 16) * n for n in range(4)]
        self.mean = [b.sbuf(f"mean{h}", [P, L + 16], at=at[h]) for h in range(2)]
        self.rinv = [b.sbuf(f"rinv{h}", [P, L + 16], at=at[2 + h]) for h in range(2)]
        self.q_scale = b.sbuf("q_scale", [P, 2, 2 * self.Q_COLS])
        self.top, self.neg_top = b.sbuf("top", [P, 2, NT]), b.sbuf("neg_top", [P, 2, NT])
        self.total, self.share = b.sbuf("total", [P, 2, NT]), b.sbuf("share", [P, 2, NT])

    LATENTS = ((range(2), 4, 256, "kv_a", 3), (range(2, 5), 6, 384, "q_a", 0))

    def latent_pe(self, e):
        b = self.b
        for k in range(6):
            b.need(e, "lat_sq", k - 1)
            b.unit(e, U_MLA + k, 1 + k, 2 * (k % 2), (b.h_hi, b.h_lo, 0),
                   before=b.h_ready(4) if k == 0 else None)
            if k:
                self.latent_total(e, k - 1)

    def latent_total(self, e, c):
        b = self.b
        tiles, bank = self.LATENTS[c >= 2][:2]
        b.need(e, "lat_sq", c + 1)
        for half in range(2):
            mm = e.matmul(b.psum[:, bank + half, 0:HALF], b.ones[:, :],
                          b.square[:, c % 2, HALF * half:HALF * half + HALF],
                          start=c == tiles[0], stop=c == tiles[-1])
        b.done(mm, "lat_total")

    def latent_act(self, e):
        b = self.b
        b.done(e.dma_start(self.table[:, :], b.ins["rope_table"]), "table", 16)

        def normed(n):
            tiles, _, _, _, to = self.LATENTS[n]
            b.rsqrt_act(e, RSQRT_LATENT + n + 1)
            for c in tiles:
                b.need(e, "lat_scaled", c + 1)
                b.step(e, e.activation(b.mix_hi[:, to + c - tiles[0], :], b.scaled[:, c % 2, :],
                                       ACT.Copy), "lat_hi", c + 1)

        for k in range(6):
            b.split_hi(e, U_MLA + k + LEAD, 1 + k + LEAD)
            b.need(e, "unit", U_MLA + k + 1)
            ps = b.both(2 * (k % 2))
            if k < 5:
                b.step(e, e.activation(halves(self.lat[:, k, :]), ps, ACT.Copy), "lat", k + 1)
                b.need(e, "lat_total", k - 1)
                b.step(e, e.activation(halves(b.square[:, k % 2, :]), ps, ACT.Square), "lat_sq",
                       k + 1)
            else:
                for h in range(2):
                    b.step(e, e.activation(halves(self.ksq[64:96, h, :]), ps[64:96], ACT.Square),
                           "kpe_sq", h + 1)
            if k == 3:
                normed(0)
        normed(1)

    def latent_dve(self, e):
        b = self.b
        b.step(e, e.tensor_scalar(b.cols[:, COLS["k_norm"]:COLS["k_norm"] + 2],
                                  b.cols[:, COLS["k_norm"]:COLS["k_norm"] + 2], QK ** -0.5, None,
                                  ALU.mult), "k_gain", 1)
        for n, (tiles, bank, width, gains, to) in enumerate(self.LATENTS):
            if n:
                b.need(e, "kpe_sq", 2)
                b.need(e, "table", 16)
                self.turn(e, 2, "k_norm", self.kpe, "kpe", 1)
            b.need(e, "lat_total", tiles[-1] + 1)
            b.rsqrt_dve(e, RSQRT_LATENT + n + 1, b.both(bank), 1.0 / width)
            for c in tiles:
                b.step(e, e.scalar_tensor_tensor(b.scaled[:, c % 2, :], self.lat[:, c, :],
                                                 b.col(gains, c - tiles[0]), b.rinv[:, 0:L],
                                                 ALU.mult, ALU.mult), "lat_scaled", c + 1)
                b.need(e, "lat_hi", c + 1)
                at = to + c - tiles[0]
                b.step(e, e.tensor_tensor(b.mix_lo[:, at, :], b.scaled[:, c % 2, :],
                                          b.mix_hi[:, at, :].bitcast(F32), ALU.subtract),
                       "lat_lo", c + 1)

    def turn(self, e, bank, gain, out, name, n):
        b = self.b
        a, s = slice(64, 96), slice(96, 128)
        other = b.scaled[a, 1, :]
        ps = b.both(bank)
        b.step(e, e.scalar_tensor_tensor(halves(out[a]), ps[a], b.col(gain, rows=a),
                                         halves(self.table[a, :]), ALU.mult, ALU.mult),
               name + "_cos", n)
        b.step(e, e.scalar_tensor_tensor(halves(other), ps[s], b.col(gain, rows=s),
                                         halves(self.table[s, :]), ALU.mult, ALU.mult),
               name + "_sin", n)
        b.step(e, e.tensor_tensor(out[a], out[a], other, ALU.add), name, n)

    def v_pe(self, e):
        b = self.b
        b.need(e, "lat_lo", 2)
        b.need(e, "kpe", 1)
        for g in range(2):
            slot = (U_MLA_V + g) % 4
            b.need(e, "w_lo", U_MLA_V + g + 1)
            for i, w in enumerate(TILES):
                b.need(e, "v2", NT * g - NT + i + 1)
                for t in range(2):
                    for n, (x, ws) in enumerate(((b.mix_hi, b.w_hi), (b.mix_lo, b.w_hi),
                                                 (b.mix_hi, b.w_lo))):
                        mm = e.matmul(b.psum[0:w, i, :], x[:, 3 + t, P * i:P * i + w],
                                      ws[:, slot, 512 * t:512 * t + 512],
                                      start=t == 0 and n == 0, stop=t == 1 and n == 2)
                b.done(mm, "v2_sum" if i < NT - 1 else "unit")

    def v_act(self, e):
        b = self.b
        for g in range(2):
            b.split_hi(e, U_MLA_V + g + LEAD, (U_MLA_V + g + LEAD) % 4)
            for i, w in enumerate(TILES):
                if i < NT - 1:
                    b.need(e, "v2_sum", (NT - 1) * g + i + 1)
                else:
                    b.need(e, "unit", U_MLA_V + g + 1)
                b.step(e, e.activation(self.v[0:w, i, 512 * g:512 * g + 512], b.psum[0:w, i, :],
                                       ACT.Copy), "v2", NT * g + i + 1)

    def pair_pe(self, e, i, j):
        b = self.b
        pair = 4 * i + j
        heads = 2 * pair
        b.need(e, "lat_lo", 5)
        b.need(e, "v2", 2 * NT)
        b.need(e, "k_done", heads)
        b.need(e, "exp2", NT * heads)
        plan = [(n, n % 3, 2 * (n // 3), n % 3 == 0, n % 3 == 2) for n in range(6)]
        plan += [(6 + n, 3 + n, 4, n == 0, n == 1) for n in range(2)]
        b.unit(e, U_PAIR + pair, 1 + j, 0, (b.mix_hi, b.mix_lo, 0), plan=plan)
        for h in range(2):
            self.totals(e, heads + h, h)
        for n in range(len(self.STEPS) + 3):
            if n < len(self.STEPS):
                self.scores(e, heads, n)
            turn = 2 <= n < len(self.STEPS) + 2
            short = turn and TILES[self.STEPS[n - 2][1]] < P
            if turn:
                self.turn_waits(e, heads, n - 2)
            if turn and not short:
                self.turn_p(e, heads, n - 2)
            if n >= 3:
                self.times_v(e, heads, n - 3)
            if short:
                self.turn_p(e, heads, n - 2)
        b.need(e, "out2", heads + 2)
        for t, w in enumerate(TILES):
            dst = b.psum[:, 6, P * t:P * t + w] if t < NT - 1 else b.psum[:, 7, 0:w]
            mm = e.transpose(dst, self.out[0:w, t, :], b.ident[0:w, 0:w])
        b.done(mm, "out_turned")

    def totals(self, e, before, h):
        b = self.b
        b.need(e, "k_squared", before + 1)
        b.need(e, "q2", before + 1)
        for half in range(2):
            bank = 2 * h + half
            e.matmul(b.psum[:, bank, 0:HALF], b.ones[0:QK, :],
                     self.ksq[0:QK, h, HALF * half:HALF * half + HALF], start=True, stop=True)
            for c in range(self.Q_COLS):
                t = self.Q_COLS * half + c
                for tile in [t] if t < NT - 1 else [0] if t >= NT else [0, t]:
                    w = TILES[tile]
                    mm = e.matmul(b.psum[0:w, bank, HALF + c:HALF + c + 1],
                                  b.square[0:QK, h, P * tile:P * tile + w], b.ones[0:QK, 0:1],
                                  start=True, stop=True)
        b.done(mm, "qk_total")

    def scores(self, e, heads, n):
        b = self.b
        h, t = self.STEPS[n]
        w, keys = TILES[t], P * t + TILES[t]
        b.need(e, "k_done", heads + h + 1)
        if n == 2:
            b.need(e, "mean", RSQRT_HEADS + heads + 2)
        if n == NT - 1:
            b.need(e, "k_raw", heads + 2)
        if h:
            b.need(e, "exp2", NT * heads + t + 1)
        q = self.q[0:QK, h, P * t:P * t + w]
        if t == NT - 1:
            e.matmul(b.psum[0:w, 4, 0:HALF], q, self.k[0:QK, h, 0:HALF], start=True, stop=True)
            e.matmul(b.psum[0:w, 5, 0:HALF], q, self.k[0:QK, h, HALF:L], start=True, stop=False)
            own = b.psum[0:w, 5, HALF - w:HALF]
        else:
            e.matmul(b.psum[0:w, t, 0:keys], q, self.k[0:QK, h, 0:keys], start=True, stop=False)
            own = b.psum[0:w, t, P * t:keys]
        b.done(e.matmul(own, b.ident16[0:w, 0:w], b.mask[0:w, 0:w], start=False, stop=True),
               "scores2")

    def turn_waits(self, e, heads, n):
        b = self.b
        count = NT * heads + n
        if n == 0:
            b.need(e, "mix3", heads)
        b.need(e, "exp2", count + 1)
        b.need(e, "pt", count)

    def turn_p(self, e, heads, n):
        b = self.b
        t = self.STEPS[n][1]
        w = TILES[t]
        for j in range(t + 1):
            r = TILES[j]
            mm = e.transpose(b.psum[0:r, 6, w * j:w * j + w], self.p[0:w, n % 2, P * j:P * j + r],
                             b.ident[0:w, 0:w])
        b.done(mm, "p_turned")

    def times_v(self, e, heads, n):
        b = self.b
        h, t = self.STEPS[n]
        w, count = TILES[t], NT * heads + n
        b.need(e, "pt", count + 1)
        b.need(e, "out2", heads + h)
        if n == 0:
            b.need(e, "v_pair", heads + 2)
        for j in range(t + 1):
            r = TILES[j]
            mm = e.matmul(b.psum[0:w, 7, 64 * t:64 * t + 64], self.pt[0:r, n % 2, w * j:w * j + w],
                          self.v2[0:r, j, 64 * h:64 * h + 64], start=j == 0, stop=j == t)
        b.done(mm, "pv")

    def pair_act(self, e, i, j):
        b = self.b
        pair = 4 * i + j
        heads = 2 * pair
        b.split_hi(e, U_PAIR + pair + LEAD, 1 + j + LEAD)
        b.need(e, "unit", U_PAIR + pair + 1)
        for h in range(2):
            n = heads + h + 1
            rows = slice(64 * h, 64 * h + 64)
            b.step(e, e.activation(halves(b.square[0:QK, h, :]), b.both(2 * h)[0:QK], ACT.Square),
                   "q_squared", n)
            b.step(e, e.activation(halves(self.k[0:64, h, :]), b.both(4)[rows], ACT.Copy,
                                   scale=b.col("k_norm", 1, rows)), "k_raw", n)
            b.step(e, e.activation(halves(self.ksq[0:64, h, :]), b.both(4)[rows], ACT.Square),
                   "k_squared", n)
        for h in range(2):
            b.ln_act(e, RSQRT_HEADS + heads + h + 1, self.mean[h], self.rinv[h], self.WIDTH)
        for h in range(2):
            b.exp_act(e, RSQRT_HEADS + heads + h + 1, self.rinv[h], self.WIDTH)
        for n, (h, t) in enumerate(self.STEPS):
            w, keys, count = TILES[t], P * t + TILES[t], NT * heads + n
            b.need(e, "top", count + 1)
            b.need(e, "p_turned", count - 1)
            dst = self.p[0:w, n % 2, 0:keys]
            last = t == NT - 1
            src = b.both(4)[0:w] if last else b.psum[0:w, t, 0:keys]
            b.done(e.activation(halves(dst) if last else dst, src, ACT.Exp,
                                bias=self.neg_top[0:w, h, t:t + 1],
                                scale=self.q_scale[0:w, h, t:t + 1],
                                accum_out=self.total[0:w, h, t:t + 1]), "exp2")
            if n:
                self.copy_pt(e, heads, n - 1)
        self.copy_pt(e, heads, n)
        b.need(e, "out_turned", pair + 1)
        full = P * (NT - 1)
        b.step(e, e.activation(b.mix_hi[:, KT + pair, 0:full], b.psum[:, 6, :], ACT.Copy),
               "mix3_hi", heads + 1)
        b.step(e, e.activation(b.mix_hi[:, KT + pair, full:L], b.psum[:, 7, 0:L - full],
                               ACT.Copy), "mix3_hi", heads + 2)

    def copy_pt(self, e, heads, n):
        b = self.b
        h, t = self.STEPS[n]
        w, count = TILES[t], NT * heads + n
        b.need(e, "p_turned", count + 1)
        b.need(e, "pv", count - 1)
        full = P if t < NT - 1 else TILES[-1]
        full *= t if t == NT - 1 else t + 1
        pt, ps = self.pt[:, n % 2, :], b.psum[:, 6, :]
        if t == NT - 1:
            b.step(e, e.activation(pt[0:w, full:full + w], ps[0:w, full:full + w], ACT.Copy),
                   "pt_tail", heads + h + 1)
        b.done(e.activation(pt[:, 0:full], ps[:, 0:full], ACT.Copy), "pt")

    def pair_dve(self, e, i, j):
        b = self.b
        pair = 4 * i + j
        heads = 2 * pair
        b.need(e, "unit", U_PAIR + pair + 1)
        for h in range(2):
            n = heads + h + 1
            b.need(e, "q_squared", n)
            b.step(e, e.tensor_scalar(halves(self.q[0:64, h, :]), b.both(2 * h)[0:64],
                                      b.col("q_norm", rows=slice(0, 64)), None, ALU.mult),
                   "q_plain", n)
            self.turn(e, 2 * h, "q_norm", self.q[:, h, :], "q2", n)
        for h in range(2):
            b.need(e, "qk_total", heads + h + 1)
            b.mean_dve(e, RSQRT_HEADS + heads + h + 1,
                       b.psum[:, 2 * h:2 * h + 2, 0:HALF + self.Q_COLS], 1.0 / QK, self.mean[h],
                       self.WIDTH)
        for h in range(2):
            n = heads + h + 1
            b.newton_dve(e, RSQRT_HEADS + n, self.mean[h], self.rinv[h], self.WIDTH)
            r = self.rinv[h][:, 0:self.WIDTH].rearrange("p (a c) -> p a c", a=2)
            b.step(e, e.tensor_copy(
                self.q_scale[:, h, :].rearrange("p (a c) -> p a c", a=2),
                r[:, :, HALF:HALF + self.Q_COLS]), "q_scale", n)
            b.step(e, e.tensor_tensor(halves(self.k[64:96, h, :]), halves(self.kpe[64:96, :]),
                                      r[64:96, :, 0:HALF], ALU.mult), "k_rot2", n)
            k = halves(self.k[0:64, h, :])
            b.step(e, e.tensor_tensor(k, k, r[0:64, :, 0:HALF], ALU.mult), "k_done", n)
        for n, (w, t) in enumerate(((P, slice(0, NT - 1)), (TILES[-1], slice(NT - 1, NT)))):
            b.step(e, e.tensor_copy(self.v2[0:w, t, :], self.v[0:w, t, bass.ds(64 * heads, P)]),
                   "v_pair", heads + n + 1)
        for n, (h, t) in enumerate(self.STEPS):
            w, keys, count = TILES[t], P * t + TILES[t], NT * heads + n
            last = t == NT - 1
            top = self.top[0:w, h, t:t + 1]
            b.need(e, "scores2", count + 1)
            if last:
                b.step(e, e.tensor_reduce(top, b.both(4)[0:w], mybir.AxisListType.XY, ALU.max),
                       "top_raw", count + 1)
            else:
                b.step(e, e.tensor_reduce(top, b.psum[0:w, t, 0:keys], AX_X, ALU.max),
                       "top_raw", count + 1)
            b.step(e, e.scalar_tensor_tensor(self.neg_top[0:w, h, t:t + 1], top, -1.0,
                                             self.q_scale[0:w, h, t:t + 1], ALU.mult, ALU.mult),
                   "top", count + 1)
            if n == NT + 1:
                self.finish(e, heads, 0)
        self.finish(e, heads, 1)
        b.need(e, "mix3_hi", heads + 2)
        full = P * (NT - 1)
        for n, (at, ps) in enumerate(((slice(0, full), b.psum[:, 6, :]),
                                      (slice(full, L), b.psum[:, 7, 0:L - full]))):
            b.step(e, e.tensor_tensor(b.mix_lo[:, KT + pair, at], ps,
                                      b.mix_hi[:, KT + pair, at].bitcast(F32), ALU.subtract),
                   "mix3", heads + n + 1)

    def finish(self, e, heads, h):
        b = self.b
        b.need(e, "pv", NT * (heads + h + 1))
        for n, (w, t, c) in enumerate(((P, slice(0, NT - 1), NT - 1),
                                       (TILES[-1], slice(NT - 1, NT), 1))):
            b.step(e, e.reciprocal(self.share[0:w, h, t], self.total[0:w, h, t]), "share",
                   2 * (heads + h) + n + 1)
            b.step(e, e.tensor_tensor(
                self.out[0:w, t, 64 * h:64 * h + 64],
                b.psum[0:w, 7, 0:64 * NT].rearrange("p (t d) -> p t d", d=64)[:, t, :],
                self.share[0:w, h, t].unsqueeze(2).to_broadcast([w, c, 64]), ALU.mult),
                *(("out2", heads + h + 1) if n else ("out_part", heads + h + 1)))

    def out_pe(self, e, i):
        b = self.b
        for j in range(4):
            m, bank = 4 * i + j, 2 * (j % 2)
            b.need(e, "k_done", 2 * PAIRS)
            b.need(e, "add", Adds.MLA + m - 1)
            b.unit(e, U_MLA_OUT + m, 1 + j, bank, (b.mix_hi, b.mix_lo, 0), None,
                   [(n, KT + n, bank, n == 0, n == 7) for n in range(8)],
                   {n: [("mix3", 2 * n + 2)] for n in range(8)} if j == 0 else None)

    def out_act(self, e, adds, i):
        for j in range(4):
            m = 4 * i + j
            self.b.split_hi(e, U_MLA_OUT + m + LEAD, 1 + j + LEAD)
            adds.act(e, Adds.MLA, m, j, 5)

    def out_dve(self, e, adds):
        adds.all_dve(e, Adds.MLA, lambda m: U_MLA_OUT + m + 1, 5)


def build(nc, ins, out):
    b = Build(nc, ins, out)
    shared = b.top
    one = Block1(b)
    b.top = shared
    ssd = Ssd(b)
    b.top = shared
    mla = Mla(b)
    adds = Adds(b)
    mlp0 = Mlp(b, adds, U_MLP0, 3, 4, 0, Adds.MLP0)
    mlp1 = Mlp(b, adds, U_MLP1, 5, None, QUARTERS, Adds.MLP1)
    gains = {n: (lambda k, n=n: b.col(("ln_mix", "ln_mlp")[(n - 2) % 2], (n - 2) // 2 * KT + k))
             for n in range(2, 6)}

    with nc.Block() as block:
        @block.sync
        def _(e):
            b.load_weights(e)
            for m in range(KT):
                b.need(e, "add", Adds.MLP1 + (QUARTERS - 1) * KT + m + 1)
                b.done(e.dma_start(out[:, m, :], b.resid[:, m, META:L]), "stored", 16)
            b.need(e, "stored", 16 * KT)

        @block.gpsimd
        def _(e):
            b.split_lo(e, 0, LEAD)
            with e.Fori(0, LAYERS1) as l:
                b.norm_pool(e, l)
                with e.Fori(0, LAYER1 // 4) as i:
                    for k in range(4):
                        b.low(e, LAYER1 * l + 4 * i + k + LEAD, k + LEAD)
                one.post_pool(e, l)
            b.norm_pool(e, 2)
            b.split_lo(e, U_DT + LEAD, U_MLP0 + LEAD)
            b.norm_pool(e, 3)
            b.split_lo(e, U_MLP0 + LEAD, U_MLA + LEAD)
            b.norm_pool(e, 4)
            b.split_lo(e, U_MLA + LEAD, U_MLP1 + LEAD)
            b.norm_pool(e, 5)
            b.split_lo(e, U_MLP1 + LEAD, UNITS)

        @block.scalar
        def _(e):
            b.done(e.dma_start(one.s[:, 0:SEQ].bitcast(I32),
                               ins["positions"].partition_broadcast(P)), "pos", 16)
            b.done(e.dma_start(b.cols[:, :], ins["cols"]), "cols", 16)
            b.done(e.dma_start(b.resid[:, :, META:L], ins["x"]), "x", 16)
            b.done(e.dma_start(b.resid[:, :, 0:META], ins["meta"]), "x", 16)
            for name, t in b.consts.items():
                b.done(e.dma_start(t[:, :], ins[name]), "const", 16)
            b.split_hi(e, 0, 0)
            b.split_hi(e, 1, 1)
            b.need(e, "cols", 16)
            b.need(e, "x", 32)
            for m in range(KT):
                b.square_act(e, 0, m, m % 2)
            one.tables_act(e)
            b.split_hi(e, 2, 2)
            with e.Fori(0, LAYERS1) as l:
                b.norm_act(e, l)
                with e.Fori(0, HEADS1) as f:
                    one.heads_act(e, l, f)
                with e.Fori(0, KT // 2) as i:
                    one.out_act(e, l, i)
                one.post_act(e, l)
            b.norm_act(e, 2)
            ssd.dt_act(e)
            ssd.project_act(e, 0, 1, range(GROUP))
            ssd.run(e, ssd.group_act)
            with e.Fori(0, KT // 2) as i:
                ssd.out_act(e, adds, i)
            b.norm_act(e, 3)
            mlp0.run(e, mlp0.up_act, mlp0.down_act)
            b.norm_act(e, 4)
            mla.latent_act(e)
            mla.v_act(e)
            with e.Fori(0, PAIRS // 4) as i:
                for j in range(4):
                    mla.pair_act(e, i, j)
            with e.Fori(0, KT // 4) as i:
                mla.out_act(e, adds, i)
            b.norm_act(e, 5)
            mlp1.run(e, mlp1.up_act, mlp1.down_act)

        @block.vector
        def _(e):
            b.step(e, e.memset(b.ssq[:, :], 0.0), "ssq_clear", 1)
            one.tables_dve(e)
            b.need(e, "x", 32)
            with e.Fori(0, LAYERS1) as l:
                b.norm_dve(e, l, lambda k: b.col("pre", l * KT + k))
                with e.Fori(0, HEADS1) as f:
                    one.heads_dve(e, l, f)
                one.out_dve(e, l)
                one.post_dve(e, l)
            b.norm_dve(e, 2, gains[2])
            ssd.dt_dve(e)
            ssd.project_dve(e, 0, range(2))
            ssd.dt_tokens(e)
            ssd.project_dve(e, 0, range(2, 4))
            ssd.run(e, ssd.group_dve)
            ssd.out_dve(e, adds)
            b.norm_dve(e, 3, gains[3])
            mlp0.run(e, mlp0.up_dve, mlp0.down_dve)
            b.norm_dve(e, 4, gains[4])
            mla.latent_dve(e)
            with e.Fori(0, PAIRS // 4) as i:
                for j in range(4):
                    mla.pair_dve(e, i, j)
            mla.out_dve(e, adds)
            b.norm_dve(e, 5, gains[5])
            mlp1.run(e, mlp1.up_dve, mlp1.down_dve)

        @block.tensor
        def _(e):
            b.head_start(e)
            events = len(b.signals)
            b.need(e, "const", 16 * len(b.consts))
            with e.Fori(0, LAYERS1) as l:
                b.norm_pe(e, l)
                with e.Fori(0, HEADS1) as f:
                    one.heads_pe(e, l, f)
                with e.Fori(0, KT // 2) as i:
                    one.out_pe(e, l, i)
                one.post_pe(e, l)
            b.norm_pe(e, 2)
            ssd.dt_pe(e)
            ssd.project_pe(e, 0, 1, range(4))
            ssd.dt_turn(e)
            ssd.project_pe(e, 0, 1, range(4, GROUP))
            ssd.run(e, ssd.group_pe)
            with e.Fori(0, KT // 2) as i:
                ssd.out_pe(e, i)
            b.norm_pe(e, 3)
            mlp0.run(e, mlp0.up_pe, mlp0.down_pe)
            b.norm_pe(e, 4)
            mla.latent_pe(e)
            mla.v_pe(e)
            with e.Fori(0, PAIRS // 4) as i:
                for j in range(4):
                    mla.pair_pe(e, i, j)
            with e.Fori(0, KT // 4) as i:
                mla.out_pe(e, i)
            b.norm_pe(e, 5)
            mlp1.run(e, mlp1.up_pe, mlp1.down_pe)
            assert len(b.signals) == events, list(b.signals)[events:]


def layout(x, positions, pre_norm, w_in, conv_w, w_out, post_norm, meta_tokens_2, ln_mix_2,
           ln_mlp_2, ssd_w_in_2, ssd_conv_w_2, ssd_conv_b_2, ssd_dt_bias_2, ssd_a_log_2, ssd_d_2,
           ssd_norm_2, ssd_w_out_2, mla_w_in_2, mla_q_a_norm_2, mla_w_q_b_2, mla_kv_a_norm_2,
           mla_w_kv_b_2, mla_q_norm_2, mla_k_norm_2, mla_w_out_2, mlp_w_up_2, mlp_w_down_2):
    f32, bf16 = np.float32, mybir.dt.np(BF16)

    def blocks(w):
        k, m = w.shape
        return w.reshape(k // P, P, m // P, P).transpose(0, 2, 1, 3)

    def tiles(v):
        return v.reshape(-1, P).T

    units = []
    for l in range(LAYERS1):
        w = blocks(w_in[l])
        for f in range(HEADS1):
            units += [w[:, KT * part + f] for part in (4, 5, 6, 1, 2, 0, 3, 7)]
        w = blocks(w_out[l])
        for m in range(KT):
            units += [w[0:KT, m], w[KT:2 * KT, m]]
    w = ssd_w_in_2[0]
    units.append(blocks(np.tile(w[:, -32:], (1, 4)))[:, 0])
    w = blocks(w[:, :-32])
    for g in range(GROUPS):
        units += [w[:, n] for n in (32 + g, 40 + g, 16 + 2 * g, 17 + 2 * g, 2 * g, 2 * g + 1)]
    w = blocks(ssd_w_out_2[0])
    for m in range(KT):
        units += [w[0:KT, m], w[KT:2 * KT, m]]

    def mlp(layer):
        up, down = blocks(mlp_w_up_2[layer]), blocks(mlp_w_down_2[layer])
        for q in range(QUARTERS):
            units.extend(up[:, KT * q + m] for m in range(KT))
            units.extend(down[KT * q:KT * q + KT, m] for m in range(KT))

    mlp(0)
    w = mla_w_in_2[0]
    rotary = w[:, -ROPE:]
    swapped = np.concatenate([rotary[:, ROPE // 2:], rotary[:, :ROPE // 2]], axis=1)
    w = blocks(np.concatenate([w[:, :-ROPE], rotary, swapped, rotary, swapped], axis=1))
    units += [w[:, n] for n in (3, 4, 0, 1, 2, 5)]
    kv = mla_w_kv_b_2[0].reshape(2, P, 2 * PAIRS, 2, 64)
    v = kv[:, :, :, 1].reshape(2, P, 2, 4, P)
    for g in range(2):
        units.append(v[:, :, g].transpose(0, 2, 1, 3).reshape(8, P, P))
    q = mla_w_q_b_2[0].reshape(3, P, 2 * PAIRS, QK)
    half = NOPE + ROPE // 2
    q = np.concatenate([q, q[..., half:], q[..., NOPE:half]], axis=3)
    k = kv[:, :, :, 0].reshape(2, P, PAIRS, P)
    for pair in range(PAIRS):
        units.append(np.concatenate([q[:, :, 2 * pair], q[:, :, 2 * pair + 1], k[:, :, pair]]))
    w = blocks(mla_w_out_2[0])
    units += [w[:, m] for m in range(KT)]
    mlp(1)
    assert len(units) == UNITS
    weights = np.stack(units).transpose(0, 2, 1, 3).reshape(UNITS, P, 8 * P)

    cols = np.zeros((P, N_COLS), f32)

    def put(name, a):
        cols[:a.shape[0], COLS[name]:COLS[name] + a.shape[1]] = a

    put("pre", tiles(pre_norm))
    put("post", tiles(post_norm))
    put("conv", conv_w.reshape(LAYERS1, 3, KT, P).transpose(3, 0, 2, 1).reshape(P, -1))
    put("ln_mix", tiles(ln_mix_2))
    put("ln_mlp", tiles(ln_mlp_2))
    freq = 1.0 / (f32(10000.0) ** (np.arange(64, dtype=f32) / f32(64)))
    put("inv_freq", np.tile(freq, 2)[:, None])
    put("sin_sign", np.repeat(f32([1, -1]), 64)[:, None])
    put("ssd_conv", ssd_conv_w_2[0].reshape(4, 32, P).transpose(2, 1, 0).reshape(P, -1))
    put("ssd_bias", tiles(ssd_conv_b_2[0]))
    put("dt_bias", np.tile(ssd_dt_bias_2[0], 4)[:, None])
    put("a_log", np.tile(ssd_a_log_2[0], 4)[:, None])
    put("ssd_d", tiles(np.repeat(ssd_d_2[0], 64)))
    put("ssd_norm", tiles(ssd_norm_2[0]))
    put("q_a", tiles(mla_q_a_norm_2[0]))
    put("kv_a", tiles(mla_kv_a_norm_2[0]))

    def with_swapped(g):
        return np.concatenate([g, g[half:], g[NOPE:half]])

    put("q_norm", with_swapped(mla_q_norm_2[0])[:, None])
    g = mla_k_norm_2[0]
    put("k_norm", np.stack([with_swapped(g), np.tile(g[:NOPE], 2)], axis=1))

    log_gamma = np.log1p(-np.exp2(-5.0 - np.arange(HEADS1)))[:, None, None]
    diff = np.arange(SEQ)[None, :] - np.arange(P)[:, None]
    decay = np.where(diff >= 0, np.exp(log_gamma * np.maximum(diff, 0)), 0.0) * P ** -0.5
    decay = np.concatenate([decay[:, :, :w] for w in WIDE1], axis=2).astype(f32)
    inv = 1.0 / (f32(10000.0) ** (np.arange(0, ROPE, 2, dtype=f32) / f32(ROPE)))
    angle = (np.arange(L, dtype=f32)[None, :] * inv[:, None]).astype(np.float64)
    table = np.zeros((P, L), f32)
    table[64:96] = np.tile(np.cos(angle), (2, 1))
    table[96:128] = np.concatenate([-np.sin(angle), np.sin(angle)])

    row, column = np.arange(P)[:, None], np.arange(P)[None, :]
    return {
        "weights": weights,
        "x": np.ascontiguousarray(x[0].reshape(SEQ, KT, P).transpose(2, 1, 0)),
        "meta": np.ascontiguousarray(meta_tokens_2.reshape(META, KT, P).transpose(2, 1, 0)),
        "positions": np.ascontiguousarray(positions[0]),
        "cols": cols,
        "decay": decay,
        "rope_table": table,
        "ones": np.ones((P, P), f32),
        "ident": np.eye(P, dtype=f32),
        "ident16": np.eye(P, dtype=f32).astype(bf16),
        "mask_t": np.where(row > column, -1e30, 0.0).astype(bf16),
        "mask": np.where(column > row, -1e30, 0.0).astype(bf16),
        "sel": (row % 32 == np.arange(32)[None, :]).astype(bf16),
    }


def kernel(**inputs):
    import concourse.bacc as bacc
    from concourse.bass_utils import run_bass_kernel_spmd

    arrays = layout(**{name: np.asarray(a) for name, a in inputs.items()})
    nc = bacc.Bacc("TRN2", target_bir_lowering=False, num_devices=1, dynamic_dma_scratch_size=1024)
    ins = {name: nc.dram_tensor("in_" + name, a.shape, mybir.dt.from_np(a.dtype),
                                kind="ExternalInput").ap() for name, a in arrays.items()}
    out = nc.dram_tensor("out", (P, KT, SEQ), F32, kind="ExternalOutput").ap()
    build(nc, ins, out)
    r = run_bass_kernel_spmd(nc, [{"in_" + name: a for name, a in arrays.items()}], core_ids=[0])
    got = r.results[0]["out"]
    return got.transpose(2, 1, 0).reshape(1, SEQ, D)
```
